# Optimizing a Trainium2 kernel written in Bass

```python
import math
import jax, jax.numpy as jnp
from jax import lax
import numpy as np

D_MODEL = 1024
BATCH = 1
SEQ = 512
DEPTH = 2

N_MIXERS = 2
QK_DIM = 64
V_DIM = 2 * QK_DIM
N_HEADS = D_MODEL // V_DIM
ROPE_DIM = QK_DIM // 4
ROPE_THETA = 500000.0
Q_BLOCK = 128
POOL_WINDOWS = (2, 4, 8, 16)
N_POOL_GROUPS = len(POOL_WINDOWS)
POOL_GROUP = D_MODEL // N_POOL_GROUPS
D_FF = 4 * D_MODEL
EPS = 1e-6
LAMBDA_STD = 0.1

kernel_name = "hybrid_diffattn_multiscale_pool_encoder"

def rmsnorm(x, g):
    xf = x.astype(jnp.float32)
    y = xf * lax.rsqrt(jnp.mean(xf * xf, axis=-1, keepdims=True) + EPS) * g.astype(jnp.float32)
    return y.astype(x.dtype)

def lambda_init_fn(layer_idx):
    return 0.8 - 0.6 * math.exp(-0.3 * layer_idx)

def rope_tables(positions):
    inv_freq = ROPE_THETA ** (-jnp.arange(0, ROPE_DIM, 2, dtype=jnp.float32) / ROPE_DIM)
    ang = positions.astype(jnp.float32)[..., None] * inv_freq
    return jnp.cos(ang)[:, None], jnp.sin(ang)[:, None]

def partial_rope(x, cos, sin):
    half = ROPE_DIM // 2
    xf = x.astype(jnp.float32)
    x1, x2, xp = xf[..., :half], xf[..., half:ROPE_DIM], xf[..., ROPE_DIM:]
    rot = jnp.concatenate([x1 * cos - x2 * sin, x2 * cos + x1 * sin, xp], axis=-1)
    return rot.astype(x.dtype)

def diff_attention(h, cos, sin, w_qkv, w_o, q_gain, k_gain, lam_q1, lam_k1, lam_q2, lam_k2,
                   sub_gain, lambda_init):
    B, S, D = h.shape
    qkv = h @ w_qkv
    q, k, v = qkv[..., :D], qkv[..., D:2 * D], qkv[..., 2 * D:]
    q = q.reshape(B, S, N_HEADS, 2, QK_DIM).transpose(3, 0, 2, 1, 4)
    k = k.reshape(B, S, N_HEADS, 2, QK_DIM).transpose(3, 0, 2, 1, 4)
    v = v.reshape(B, S, N_HEADS, V_DIM).transpose(0, 2, 1, 3)
    q = partial_rope(rmsnorm(q, q_gain), cos, sin)
    k = partial_rope(rmsnorm(k, k_gain), cos, sin)
    scale = 1.0 / math.sqrt(QK_DIM)
    lam = (jnp.exp(jnp.sum(lam_q1.astype(jnp.float32) * lam_k1.astype(jnp.float32)))
           - jnp.exp(jnp.sum(lam_q2.astype(jnp.float32) * lam_k2.astype(jnp.float32)))
           + lambda_init)
    n_blk = S // Q_BLOCK
    qb = q.reshape(2, B, N_HEADS, n_blk, Q_BLOCK, QK_DIM).transpose(3, 0, 1, 2, 4, 5)

    def attend_block(q_blk):
        s = jnp.einsum('mbhqd,mbhkd->mbhqk', q_blk, k).astype(jnp.float32) * scale
        p = jax.nn.softmax(s, axis=-1)
        a = p[0] - lam * p[1]
        return jnp.einsum('bhqk,bhkv->bhqv', a.astype(v.dtype), v)

    o = lax.map(attend_block, qb)
    o = o.transpose(1, 2, 0, 3, 4).reshape(B, N_HEADS, S, V_DIM)
    o = rmsnorm(o, sub_gain) * (1.0 - lambda_init)
    o = o.transpose(0, 2, 1, 3).reshape(B, S, N_HEADS * V_DIM)
    return o @ w_o

def multiscale_pool(h, w_group, ch_scale):
    B, S, D = h.shape
    hf = h.astype(jnp.float32)
    cs = jnp.concatenate([jnp.zeros((B, 1, D), jnp.float32), jnp.cumsum(hf, axis=1)], axis=1)
    t = jnp.arange(S)
    pooled = []
    for g, w in enumerate(POOL_WINDOWS):
        lo = jnp.clip(t - w // 2, 0, S)
        hi = jnp.clip(t + w // 2, 0, S)
        csg = cs[..., g * POOL_GROUP:(g + 1) * POOL_GROUP]
        tot = jnp.take(csg, hi, axis=1) - jnp.take(csg, lo, axis=1)
        cnt = (hi - lo).astype(jnp.float32)[None, :, None]
        pooled.append(tot / cnt)
    mean = jnp.concatenate(pooled, axis=-1)
    diff = (mean - hf).astype(h.dtype).reshape(B, S, N_POOL_GROUPS, POOL_GROUP)
    y = jnp.einsum('bsgc,gcd->bsgd', diff, w_group).reshape(B, S, D)
    return y * ch_scale

def sqrelu_mlp(h, w1, w2):
    return jnp.square(jax.nn.relu(h @ w1)) @ w2

def setup_inputs(seed: int = 0) -> dict:
    key = jax.random.key(seed)
    ks = jax.random.split(key, 20)
    n_attn = (DEPTH + N_MIXERS - 1) // N_MIXERS
    n_pool = DEPTH // N_MIXERS
    f32 = jnp.float32
    nrm = lambda k, shape, s: jax.random.normal(k, shape, f32) * s
    x = jax.random.normal(ks[0], (BATCH, SEQ, D_MODEL), f32)
    offsets = jax.random.randint(ks[1], (BATCH, 1), 0, 4096, dtype=jnp.int32)
    positions = (offsets + jnp.arange(SEQ, dtype=jnp.int32)[None, :]).astype(jnp.int32)
    return {
        "x": x,
        "positions": positions,
        "norm_mix": 1.0 + nrm(ks[2], (DEPTH, D_MODEL), 0.05),
        "norm_mlp": 1.0 + nrm(ks[3], (DEPTH, D_MODEL), 0.05),
        "attn_w_qkv": nrm(ks[4], (n_attn, D_MODEL, 3 * D_MODEL), D_MODEL ** -0.5),
        "attn_w_o": nrm(ks[5], (n_attn, N_HEADS * V_DIM, D_MODEL), (N_HEADS * V_DIM) ** -0.5),
        "attn_q_gain": 1.0 + nrm(ks[6], (n_attn, QK_DIM), 0.05),
        "attn_k_gain": 1.0 + nrm(ks[7], (n_attn, QK_DIM), 0.05),
        "attn_lam_q1": nrm(ks[8], (n_attn, QK_DIM), LAMBDA_STD),
        "attn_lam_k1": nrm(ks[9], (n_attn, QK_DIM), LAMBDA_STD),
        "attn_lam_q2": nrm(ks[10], (n_attn, QK_DIM), LAMBDA_STD),
        "attn_lam_k2": nrm(ks[11], (n_attn, QK_DIM), LAMBDA_STD),
        "attn_sub_gain": 1.0 + nrm(ks[12], (n_attn, V_DIM), 0.05),
        "pool_w": nrm(ks[13], (n_pool, N_POOL_GROUPS, POOL_GROUP, POOL_GROUP), POOL_GROUP ** -0.5),
        "pool_scale": 0.5 + nrm(ks[14], (n_pool, D_MODEL), 0.05),
        "mlp_w1": nrm(ks[15], (DEPTH, D_MODEL, D_FF), D_MODEL ** -0.5),
        "mlp_w2": nrm(ks[16], (DEPTH, D_FF, D_MODEL), D_FF ** -0.5),
    }

def reference(x, positions, norm_mix, norm_mlp, attn_w_qkv, attn_w_o, attn_q_gain, attn_k_gain,
              attn_lam_q1, attn_lam_k1, attn_lam_q2, attn_lam_k2, attn_sub_gain,
              pool_w, pool_scale, mlp_w1, mlp_w2):
    cos, sin = rope_tables(positions)
    for i in range(DEPTH):
        j = i // N_MIXERS
        h = rmsnorm(x, norm_mix[i])
        if i % N_MIXERS == 0:
            y = diff_attention(h, cos, sin, attn_w_qkv[j], attn_w_o[j], attn_q_gain[j], attn_k_gain[j],
                               attn_lam_q1[j], attn_lam_k1[j], attn_lam_q2[j], attn_lam_k2[j],
                               attn_sub_gain[j], lambda_init_fn(i))
        else:
            y = multiscale_pool(h, pool_w[j], pool_scale[j])
        x = x + y.astype(x.dtype)
        h = rmsnorm(x, norm_mlp[i])
        x = x + sqrelu_mlp(h, mlp_w1[i], mlp_w2[i]).astype(x.dtype)
    return x


_drawn_inputs = setup_inputs


def setup_inputs(seed=0):
    import zlib

    import numpy as np

    out = dict(_drawn_inputs(seed))
    spreads = {}
    factors = {'attn_lam_k1': 8.0, 'attn_lam_q2': 8.0}
    for name, (base, spread) in spreads.items():
        noise = np.random.default_rng([zlib.crc32(name.encode()), seed]).standard_normal(out[name].shape)
        drawn = base * np.exp(spread * noise) if base else spread * noise
        out[name] = __import__('jax').numpy.asarray(drawn.astype(out[name].dtype))
    for name, factor in factors.items():
        out[name] = (out[name] * factor).astype(out[name].dtype)
    return out
```

```python
import math
from contextlib import ExitStack

import numpy as np

import concourse.bass as bass
from concourse import mybir

F32 = mybir.dt.float32
F32R = mybir.dt.float32r
I32 = mybir.dt.int32
ALU = mybir.AluOpType
ACT = mybir.ActivationFunctionType
AX = mybir.AxisListType

P = 128
D = 1024
S = 512
DFF = 4096
QK = 64
VD = 128
NH = D // VD
ROPE = QK // 4
HALF = ROPE // 2
THETA = 500000.0
WINDOWS = (2, 4, 8, 16)
NG = len(WINDOWS)
GW = D // NG
EPS = 1e-6
NC = D // P
NT = S // P
BANK = 512
SLAB = 8 * BANK
PIECE = SLAB // 4
FB = 512
NB = DFF // FB
CH = FB // P
LAMBDA_INIT = 0.8 - 0.6 * math.exp(-0.3 * 0)
PAD = max(WINDOWS) // 2
BW = P + 2 * PAD

WO0 = 6
MLP0 = WO0 + 2
POOLS = MLP0 + 2 * NB
MLP1 = POOLS + 1
NSLAB = MLP1 + 2 * NB
MLP_SLAB = (MLP0, MLP1)
Y_MLP = (16, 16 + 8 * NB)


def build_trunk(nc, x, positions, norm_mix, norm_mlp, w_qkv, w_o, q_gain, k_gain, lam_q1, lam_k1,
                lam_q2, lam_k2, sub_gain, pool_w, pool_scale, w1, w2, out):
    ctx = ExitStack()
    with ctx:
        cursor = [-(-nc.sbuf_base // 32) * 32]

        def at(name, shape, dt, offset):
            return nc.alloc_sbuf_tensor_at("s_" + name, shape, dt, offset=offset)

        def size(shape):
            n = 4
            for k in shape[1:]:
                n *= k
            return -(-n // 32) * 32

        def sb(name, shape, dt=F32):
            t = at(name, shape, dt, cursor[0])
            cursor[0] += size(shape)
            return t

        def region(kbytes):
            base = cursor[0]
            cursor[0] += kbytes * 1024
            return base

        def inside(base, *wanted):
            made = []
            for name, shape, dt in wanted:
                made.append(at(name, shape, dt, base))
                base += size(shape)
            return made

        def sem(name):
            return ctx.enter_context(nc.semaphore(name))

        raw = [sb(f"raw{k}", [P, PIECE]) for k in range(4)]
        w_hi = [sb(f"w_hi{k}", [P, SLAB], F32R) for k in range(2)]
        w_lo = [sb(f"w_lo{k}", [P, SLAB], F32R) for k in range(2)]
        xT = sb("xT", [P, NC, S])
        h_region = region(32)
        qk_region = region(32)
        v_region = region(32)
        qkT_hi = [[sb(f"{n}T_hi{k}", [P, S], F32R) for k in range(2)] for n in "qk"]
        qkT_lo = [[sb(f"{n}T_lo{k}", [P, S], F32R) for k in range(2)] for n in "qk"]

        hT_hi, hT_lo = inside(h_region, ("hT_hi", [P, NC, S], F32R), ("hT_lo", [P, NC, S], F32R))
        aT_hi, aT_lo, p0, p1, oc, osq, odiag = inside(
            h_region, ("aT_hi", [P, NT, S], F32R), ("aT_lo", [P, NT, S], F32R),
            ("p0", [P, 2, S], F32), ("p1", [P, 2, S], F32), ("oc", [P, S], F32),
            ("osq", [P, S], F32), ("odiag", [P, NT, P], F32))
        probs = [p0, p1]
        (qkn,) = inside(qk_region, ("qkn", [P, NH, 2, NT, P], F32))
        oT = inside(qk_region, *[(f"oT{h}", [P, 2, S], F32R) for h in range(NH)])
        uT_hi, uT_lo, z, zz, r_bc, nsum, nsq = inside(
            qk_region, ("uT_hi", [P, CH, S], F32R), ("uT_lo", [P, CH, S], F32R),
            ("z", [P, 2, S], F32), ("zz", [P, 2, S], F32), ("r_bc", [P, S], F32),
            ("nsum", [P, S], F32), ("nsq", [P, 2, S], F32))
        zn_hi, zn_lo = inside(qk_region, ("zn_hi", [P, 2, NT, GW], F32R), ("zn_lo", [P, 2, NT, GW], F32R))
        (onat,) = inside(qk_region, ("onat", [P, 4, NT, P], F32))
        v_hi, v_lo = inside(v_region, ("v_hi", [P, NT, D], F32R), ("v_lo", [P, NT, D], F32R))
        x_nat, hn, g_bc, lam_in, lam_t, ropet = inside(
            v_region, ("x_nat", [P, NT, D], F32), ("hn", [P, 2, D], F32), ("g_bc", [P, D], F32),
            ("lam_in", [P, 4, QK], F32), ("lam_t", [P, 2, QK], F32), ("ropet", [P, 16, NT * HALF], F32))
        band_f, band, inv_cnt = inside(
            v_region, ("band_f", [P, NG, NT, BW], F32), ("band", [P, NG, NT, BW], F32R),
            ("inv_cnt", [P, NG, S], F32))
        qs = [at(f"qs{k}", [P, S], F32, qkT_base) for k, qkT_base in
              enumerate((cursor[0] - 16 * 1024, cursor[0] - 14 * 1024))]
        qsq = [at(f"qsq{k}", [P, S], F32, cursor[0] - (12 - 2 * k) * 1024) for k in range(2)]
        rt = [at(f"rt{k}", [P, 2 * NT, ROPE], F32, cursor[0] - (8 - k) * 1024) for k in range(4)]

        ident = sb("ident", [P, P])
        ones = sb("ones", [P, P])
        rope_c = [sb(f"rope_c{n}", [P, NT, ROPE]) for n in "qk"]
        rope_s = [sb(f"rope_s{n}", [P, NT, ROPE]) for n in "qk"]
        minus_half = sb("minus_half", [P, 8])
        gcol = sb("gcol", [P, 4, NC])
        qk_col = sb("qk_col", [P, 2])
        sub_col = sb("sub_col", [P, 1])
        neg_lam = sb("neg_lam", [P, 1])
        lam_e = sb("lam_e", [P, 4])
        st_ss = sb("st_ss", [P, 8])
        st_v = sb("st_v", [P, 8])
        st_r = sb("st_r", [P, 8])
        qk_ss = sb("qk_ss", [P, 2, 8])
        qk_v = sb("qk_v", [P, 2, 8])
        qk_r = sb("qk_r", [P, 2, 8])
        nmax = sb("nmax", [P, 2, 2])
        lsum = sb("lsum", [P, 2, 2])
        rl = sb("rl", [P, 2, 2])
        mixc = sb("mixc", [P, 2, 1])
        rl0 = sb("rl0", [P, NH * NT])
        o_v = sb("o_v", [P, 4 * NT])
        o_r = sb("o_r", [P, 2 * NT])
        posi = sb("posi", [P, NT], I32)
        posf = sb("posf", [P, NT])
        rope_g = sb("rope_g", [P, 2, ROPE])
        assert cursor[0] <= nc.sbuf_usable_end, (cursor[0], nc.sbuf_usable_end)

        bank = [ctx.enter_context(nc.psum_tensor(f"bank{k}", [P, BANK], F32)) for k in range(8)]

        x_loaded = [sem(f"x_loaded{k}") for k in range(NT)]
        small_loaded = sem("small_loaded")
        gains_loaded = sem("gains_loaded")
        raw_loaded = [sem(f"raw_loaded{k}") for k in range(4)]
        stored = [sem(f"stored{k}") for k in range(4)]
        w_hi_done = sem("w_hi_done")
        w_lo_done = sem("w_lo_done")
        consts = sem("consts")
        cols_ready = sem("cols_ready")
        sq_done = sem("sq_done")
        v_done = sem("v_done")
        r_done = sem("r_done")
        hn_done = sem("hn_done")
        x_turned = sem("x_turned")
        x_kept = sem("x_kept")
        hn_turned = sem("hn_turned")
        h_hi_done = sem("h_hi_done")
        h_lo_done = sem("h_lo_done")
        proj_done = sem("proj_done")
        qk_copied = sem("qk_copied")
        qk_squared = sem("qk_squared")
        qk_v_done = sem("qk_v_done")
        qk_r_done = sem("qk_r_done")
        qk_ready = sem("qk_ready")
        v_hi_done = sem("v_hi_done")
        v_lo_done = sem("v_lo_done")
        rope_dve = sem("rope_dve")
        rope_act = sem("rope_act")
        lam_exp = sem("lam_exp")
        qk_turned = sem("qk_turned")
        qkT_hi_done = sem("qkT_hi_done")
        qkT_lo_done = sem("qkT_lo_done")
        scored = sem("scored")
        max_done = sem("max_done")
        exp_done = sem("exp_done")
        a_done = sem("a_done")
        a_turned = sem("a_turned")
        aT_hi_done = sem("aT_hi_done")
        aT_lo_done = sem("aT_lo_done")
        pv_done = sem("pv_done")
        o_copied = sem("o_copied")
        o_squared = sem("o_squared")
        o_summed = sem("o_summed")
        o_v_done = sem("o_v_done")
        o_r_done = sem("o_r_done")
        o_diag_done = sem("o_diag_done")
        o_spread = sem("o_spread")
        o_normed = sem("o_normed")
        oT_hi_done = sem("oT_hi_done")
        oT_lo_done = sem("oT_lo_done")
        y_ready = sem("y_ready")
        y_added = sem("y_added")
        n_hi = sem("n_hi")
        n_lo = sem("n_lo")
        n_squared = sem("n_squared")
        n_summed = sem("n_summed")
        n_stat = sem("n_stat")
        n_v = sem("n_v")
        n_r = sem("n_r")
        n_diag = sem("n_diag")
        n_spread = sem("n_spread")
        n_rbc = sem("n_rbc")
        h1_ready = sem("h1_ready")
        z_done = sem("z_done")
        u_hi_done = sem("u_hi_done")
        zz_done = sem("zz_done")
        u_lo_done = sem("u_lo_done")
        zn_ready = sem("zn_ready")
        zn_hi_done = sem("zn_hi_done")
        zn_lo_done = sem("zn_lo_done")
        band_ready = sem("band_ready")
        pooled = sem("pooled")
        pool_added = sem("pool_added")
        out_turned = sem("out_turned")
        out_kept = sem("out_kept")
        dve_chain = sem("dve_chain")
        pool_chain = sem("pool_chain")

        def wait_used(eng, s):
            if s < 0:
                return
            if s < WO0:
                eng.wait_ge(proj_done, NT * (s + 1))
            elif s < MLP0:
                eng.wait_ge(y_ready, NC * (s - WO0 + 1))
            elif s == POOLS:
                eng.wait_ge(zn_ready, NG)
            else:
                layer = int(s > POOLS)
                j, down = divmod(s - MLP_SLAB[layer], 2)
                if down:
                    eng.wait_ge(y_ready, Y_MLP[layer] + NC * (j + 1))
                else:
                    eng.wait_ge(h1_ready, CH * (NB * layer + j + 1))

        def f32(ap):
            return ap.bitcast(F32)

        def piece(slab, k):
            if slab < WO0:
                n0 = slab // 2 * D + slab % 2 * BANK
                return w_qkv.rearrange("(c p) n -> p c n", p=P)[:, 2 * k:2 * k + 2, n0:n0 + BANK]
            if slab < MLP0:
                return w_o.rearrange("(c p) n -> p c n", p=P)[:, 4 * (slab - WO0) + k, :]
            assert slab == POOLS
            return pool_w[k].rearrange("(c p) n -> p c n", p=P)

        def w1_piece(layer, j, k):
            return w1[layer].rearrange("(c p) n -> p c n", p=P)[:, 2 * k:2 * k + 2, bass.ds(j * FB, FB)]

        def w2_piece(layer, j, k):
            return w2[layer].rearrange("(b k p) n -> p k b n", p=P, k=CH)[:, k, bass.ds(j, 1), :]

        block = ctx.enter_context(nc.Block())

        @block.sync
        def _(sp):
            xv = x.rearrange("a (t p) d -> p (a t) d", p=P)
            for t in range(NT):
                sp.dma_start(x_nat[:, t, :], xv[:, t, :]).then_inc(x_loaded[t], 16)

            def load(slab, k, src, width=PIECE):
                if not isinstance(slab, int) or slab >= 1:
                    sp.wait_ge(w_lo_done, slab * 4 + (k - 3))
                dst = raw[k][:, 0:width]
                if len(src.shape) == 3:
                    dst = dst.rearrange("p (a b) -> p a b", a=src.shape[1])
                sp.dma_start(dst, src).then_inc(raw_loaded[k], 16)

            for s in range(MLP0):
                for k in range(4):
                    load(s, k, piece(s, k))
            for layer in range(2):
                base = MLP_SLAB[layer]
                if layer:
                    for k in range(4):
                        load(POOLS, k, piece(POOLS, k), 2 * GW)
                for k in range(4):
                    load(base, k, w1_piece(layer, 0, k))
                with sp.Fori(0, NB - 1) as j:
                    for k in range(4):
                        load(j * 2 + (base + 1), k, w2_piece(layer, j, k))
                    for k in range(4):
                        load(j * 2 + (base + 2), k, w1_piece(layer, j + 1, k))
                for k in range(4):
                    load(base + 2 * NB - 1, k, w2_piece(layer, NB - 1, k))
            ov = out.rearrange("a (t p) d -> p (a t) d", p=P)
            for c in range(NC):
                sp.wait_ge(out_kept, c + 1)
                sp.dma_start(ov[:, :, c * P:(c + 1) * P], onat[:, c % 4, :, :]).then_inc(stored[c % 4], 16)
            for k in range(4):
                sp.wait_ge(stored[k], 16 * (NC // 4))

        @block.gpsimd
        def _(pool):
            g = nc.gpsimd
            links = [0]

            def link(ins):
                links[0] += 1
                ins.then_inc(pool_chain, 1)
                pool.wait_ge(pool_chain, links[0])

            g.memset(minus_half[:], -0.5).then_inc(consts, 1)
            g.memset(ones[:], 1.0).then_inc(consts, 1)
            link(g.memset(ident[:], 0.0))
            g.affine_select(out=ident[:], in_=ident[:], compare_op=ALU.not_equal, fill=1.0, base=0,
                            pattern=[[-1, P]], channel_multiplier=1).then_inc(consts, 1)
            pool.wait_ge(consts, 1)

            for t in range(NT):
                pool.wait_ge(v_done, t + 1)
                g.tensor_tensor(st_r[:, t:t + 1], st_v[:, t:t + 1], minus_half[:, 0:1], ALU.pow)\
                    .then_inc(r_done, 1)
            for n in range(16):
                pool.wait_ge(qk_copied, n + 1)
                if n >= 2:
                    pool.wait_ge(qk_v_done, n - 1)
                g.tensor_tensor(qsq[n % 2][:], qs[n % 2][:], qs[n % 2][:], ALU.mult).then_inc(qk_squared, 1)
                pool.wait_ge(qk_v_done, n + 1)
                if n >= 2:
                    pool.wait_ge(qk_ready, n - 1)
                g.tensor_tensor(qk_r[:, n % 2, :], qk_v[:, n % 2, :], minus_half[:], ALU.pow)\
                    .then_inc(qk_r_done, 1)
            for h in range(NH):
                pool.wait_ge(o_v_done, h + 1)
                if h >= 2:
                    pool.wait_ge(o_diag_done, h - 1)
                s0 = h % 2 * NT
                g.tensor_tensor(o_r[:, s0:s0 + NT], o_v[:, 2 * s0:2 * s0 + NT], minus_half[:, 0:NT], ALU.pow)\
                    .then_inc(o_r_done, 1)

            def norm(m):
                for c in range(NC):
                    pool.wait_ge(n_squared, NC * m + c + 1)
                    if c == 0:
                        if m:
                            pool.wait_ge(n_stat, m)
                        continue
                    first = nsq[:, 0, :] if c == 1 else nsum[:]
                    if c >= 2:
                        pool.wait_ge(n_summed, (NC - 1) * m + c - 1)
                    g.tensor_tensor(nsum[:], first, nsq[:, c % 2, :], ALU.add).then_inc(n_summed, 1)
                pool.wait_ge(n_v, m + 1)
                g.tensor_tensor(st_r[:, 0:NT], st_v[:, 0:NT], minus_half[:, 0:NT], ALU.pow).then_inc(n_r, 1)

            norm(0)
            for gi, w in enumerate(WINDOWS):
                hw = w // 2
                v = band_f[:, gi, :, :]
                link(g.memset(v, 1.0))
                link(g.affine_select(out=v, in_=v, compare_op=ALU.is_ge, fill=0.0, base=PAD + hw,
                                     pattern=[[0, NT], [-1, BW]], channel_multiplier=1))
                link(g.affine_select(out=v, in_=v, compare_op=ALU.is_gt, fill=0.0, base=hw - PAD,
                                     pattern=[[0, NT], [1, BW]], channel_multiplier=-1))
                link(g.affine_select(out=v, in_=v, compare_op=ALU.not_equal, fill=float(1 - w), base=PAD,
                                     pattern=[[0, NT], [-1, BW]], channel_multiplier=1))
                link(g.memset(inv_cnt[:, gi, :], 1.0 / w))
                for t in [*range(hw), *range(S - hw + 1, S)]:
                    cnt = min(t + hw, S) - max(t - hw, 0)
                    tile, col = t // P, t % P + PAD
                    one = band_f[:, gi, tile, col:col + 1]
                    g.affine_select(out=one, in_=one, compare_op=ALU.not_equal, fill=float(1 - cnt),
                                    base=-(t % P), pattern=[[0, 1]], channel_multiplier=1)
                    link(g.memset(inv_cnt[:, gi, t:t + 1], float(np.float32(1.0) / np.float32(cnt))))
            g.tensor_copy(band[:], band_f[:]).then_inc(band_ready, 1)
            norm(1)
            norm(2)

        @block.scalar
        def _(act):
            a = nc.scalar
            with nc.allow_non_contiguous_dma("gains as columns, a few KB"):
                act.dma_start(posi[:], positions.rearrange("a (t p) -> p (a t)", p=P)).then_inc(small_loaded, 16)
                for n, gain in enumerate((q_gain, k_gain)):
                    act.dma_start(rope_g[:, n, :], gain[0:ROPE].partition_broadcast(P)).then_inc(small_loaded, 16)
                for n, lam in enumerate((lam_q1, lam_k1, lam_q2, lam_k2)):
                    act.dma_start(lam_in[:, n, :], lam.partition_broadcast(P)).then_inc(small_loaded, 16)
                act.dma_start(g_bc[:], norm_mix[0].partition_broadcast(P)).then_inc(small_loaded, 16)
                for n, col in enumerate((norm_mlp[0], norm_mix[1], norm_mlp[1], pool_scale)):
                    act.dma_start(gcol[:, n, :], col.rearrange("(c p) -> p c", p=P)).then_inc(gains_loaded, 16)
                act.dma_start(sub_col[:], sub_gain.rearrange("(p a) -> p a", a=1)).then_inc(gains_loaded, 16)
                act.wait_ge(cols_ready, 1)
                for n, gain in enumerate((q_gain, k_gain)):
                    for m in range(2):
                        act.dma_start(qk_col[m * QK + ROPE:(m + 1) * QK, n:n + 1],
                                      gain[ROPE:QK].rearrange("(p a) -> p a", a=1)).then_inc(gains_loaded, 16)

            act.wait_ge(rope_dve, 1)
            a.activation(ropet[:, 2:4, :], ropet[:, 0:2, :], ACT.Sin).then_inc(rope_act, 1)
            act.wait_ge(lam_exp, 1)
            a.activation(lam_e[:, 0:2], lam_e[:, 2:4], ACT.Exp).then_inc(rope_act, 1)

            def split_hi(s, k, slot, width=PIECE, free=None):
                act.wait_ge(raw_loaded[k], s * 16 + 16)
                if free is not None:
                    free()
                else:
                    wait_used(act, s - 2)
                a.activation(w_hi[slot][:, k * width:(k + 1) * width], raw[k][:, 0:width], ACT.Copy)\
                    .then_inc(w_hi_done, 1)

            def input_squares(t):
                act.wait_ge(x_loaded[t], 16)
                if t >= 2:
                    act.wait_ge(hn_turned, 2 * (t - 1))
                a.activation(hn[:, t % 2, :], x_nat[:, t, :], ACT.Square, accum_out=st_ss[:, t:t + 1])\
                    .then_inc(sq_done, 1)

            def keep_x(n):
                t, half = n // 2, n % 2
                act.wait_ge(x_turned, n + 1)
                a.activation(xT[:, 4 * half:4 * half + 4, t * P:(t + 1) * P],
                             bank[n % 4][:].rearrange("p (c t) -> p c t", c=4), ACT.Copy).then_inc(x_kept, 1)

            def h_hi(n):
                t, half = n // 2, n % 2
                act.wait_ge(hn_turned, n + 1)
                a.activation(hT_hi[:, 4 * half:4 * half + 4, t * P:(t + 1) * P],
                             bank[4 + n % 4][:].rearrange("p (c t) -> p c t", c=4), ACT.Copy)\
                    .then_inc(h_hi_done, 1)

            input_squares(0)
            input_squares(1)
            for t in range(NT):
                keep_x(2 * t)
                keep_x(2 * t + 1)
                h_hi(2 * t)
                h_hi(2 * t + 1)
                if t + 2 < NT:
                    input_squares(t + 2)
                split_hi(0, t, 0)

            for s in range(WO0):
                for t in range(NT):
                    split_hi(s + 1, t, (s + 1) % 2)
                    n = NT * s + t
                    act.wait_ge(proj_done, n + 1)
                    if s < 4:
                        if n >= 2:
                            act.wait_ge(qk_ready, n - 1)
                        a.activation(qs[n % 2][:], bank[n % 4][:], ACT.Copy).then_inc(qk_copied, 1)
                    else:
                        cols = slice((s - 4) * BANK, (s - 3) * BANK)
                        a.activation(v_hi[:, t, cols], bank[n % 4][:], ACT.Copy).then_inc(v_hi_done, 1)

            def qkT(h):
                for n in range(2):
                    act.wait_ge(qk_turned, 2 * h + n + 1)
                    if h >= 2:
                        act.wait_ge(scored, NT * (h - 1))
                    elif h == 0 and n == 0:
                        act.wait_ge(qk_ready, 16)
                    a.activation(qkT_hi[n][h % 2][:], bank[6 + n][:], ACT.Copy, scale=qk_col[:, n:n + 1])\
                        .then_inc(qkT_hi_done, 1)

            act.wait_ge(gains_loaded, 16 * 9)
            act.wait_ge(cols_ready, 2)
            qkT(0)
            for i in range(NH * NT + 5):
                if i < NH * NT:
                    act.wait_ge(max_done, i + 1)
                    if i >= 2:
                        act.wait_ge(a_turned, i - 1)
                    else:
                        wait_used(act, WO0 - 1)
                    for m in range(2):
                        a.activation(probs[i % 2][:, m, :], bank[2 * (i % 2) + m][:], ACT.Exp,
                                     bias=nmax[:, i % 2, m:m + 1],
                                     accum_out=lsum[:, i % 2, m:m + 1]).then_inc(exp_done, 1)
                if 1 <= i <= NH * NT:
                    h, t = divmod(i - 1, NT)
                    act.wait_ge(a_turned, i)
                    if t == 0 and h:
                        act.wait_ge(pv_done, h)
                    a.activation(aT_hi[:, :, t * P:(t + 1) * P], bank[4][:].rearrange("p (k t) -> p k t", k=NT),
                                 ACT.Copy).then_inc(aT_hi_done, 1)
                if i % NT == 2 and i // NT + 1 < NH:
                    qkT(i // NT + 1)
                if i >= 5 and (i - 5) % NT == 0:
                    h = (i - 5) // NT
                    act.wait_ge(pv_done, h + 1)
                    if h:
                        act.wait_ge(oT_lo_done, h)
                        act.wait_ge(o_summed, h)
                    a.activation(oc[:], bank[5][:], ACT.Copy).then_inc(o_copied, 1)
                    a.activation(osq[:], bank[5][:], ACT.Square).then_inc(o_squared, 1)
                if i >= 7 and (i - 7) % NT == 0:
                    h = (i - 7) // NT
                    act.wait_ge(o_normed, h + 1)
                    a.activation(oT[h][:, 0, :], oc[:], ACT.Copy, scale=sub_col[:, 0:1]).then_inc(oT_hi_done, 1)

            for s in range(WO0, MLP0):
                for k in range(4):
                    split_hi(s + 1, k, (s + 1) % 2)

            def norm(m, before):
                done, count = before
                for c in range(NC):
                    act.wait_ge(done, count - NC + c + 1)
                    a.activation(hT_hi[:, c, :], xT[:, c, :], ACT.Copy, scale=gcol[:, m, c:c + 1])\
                        .then_inc(n_hi, 1)
                for c in range(NC):
                    if m or c >= 2:
                        act.wait_ge(n_summed, (NC - 1) * m + (max(1, c - 2) if c >= 2 else 0))
                    a.activation(nsq[:, c % 2, :], xT[:, c, :], ACT.Square).then_inc(n_squared, 1)

            def spread_copy(m):
                act.wait_ge(n_spread, m + 1)
                a.activation(r_bc[:], bank[6][:], ACT.Copy).then_inc(n_rbc, 1)

            def up_phase(s, slot, b, after_split=None):
                def split(f):
                    split_hi(s + 1, f, 1 - slot, free=lambda: act.wait_ge(y_ready, b * NC + Y_MLP[0]))

                if after_split is not None:
                    for f in range(CH):
                        split(f)
                    after_split()
                for f in range(CH):
                    if after_split is None:
                        split(f)
                    act.wait_ge(z_done, b * CH + (f + 1))
                    a.activation(uT_hi[:, f, :], z[:, f % 2, :], ACT.Square).then_inc(u_hi_done, 1)
                    a.activation(zz[:, f % 2, :], z[:, f % 2, :], ACT.Square).then_inc(zz_done, 1)

            def down_phase(s, slot, b, width=PIECE):
                for k in range(4):
                    split_hi(s + 1, k, 1 - slot, width, free=lambda: act.wait_ge(h1_ready, b * CH + CH))

            for layer in range(2):
                base = MLP_SLAB[layer]
                slot = base % 2
                if layer == 0:
                    norm(0, (y_added, 16))
                else:
                    norm(1, (y_added, Y_MLP[1]))
                    for k in range(4):
                        split_hi(MLP1, k, MLP1 % 2)
                    act.wait_ge(n_r, 2)
                    for gi in range(NG):
                        act.wait_ge(zn_ready, gi + 1)
                        if gi >= 2:
                            act.wait_ge(pooled, 2 * (gi - 1))
                        for t in range(NT):
                            a.activation(zn_hi[:, gi % 2, t, :], bank[2 * gi + t // 2][:, t % 2 * GW:(t % 2 + 1) * GW],
                                         ACT.Copy, scale=st_r[:, t:t + 1]).then_inc(zn_hi_done, 1)
                    norm(2, (pool_added, NC))
                up_phase(base, slot, NB * layer, lambda: spread_copy(layer))
                with act.Fori(0, NB - 1) as j:
                    down_phase(j * 2 + (base + 1), 1 - slot, j + NB * layer)
                    up_phase(j * 2 + (base + 2), slot, j + (NB * layer + 1))
                if layer == 0:
                    down_phase(base + 2 * NB - 1, 1 - slot, NB - 1, 2 * GW)
            for c in range(NC):
                act.wait_ge(out_turned, c + 1)
                if c >= 4:
                    act.wait_ge(stored[c % 4], 16 * (c // 4))
                a.activation(onat[:, c % 4, :, :], bank[c % 4][:].rearrange("p (t c) -> p t c", t=NT), ACT.Copy)\
                    .then_inc(out_kept, 1)

        @block.vector
        def _(dve):
            v = nc.vector
            links = [0]

            def link(ins):
                links[0] += 1
                ins.then_inc(dve_chain, 1)
                dve.wait_ge(dve_chain, links[0])

            v.memset(qk_col[:], 1.0).then_inc(cols_ready, 1)
            dve.wait_ge(small_loaded, 16 * 8)
            link(v.tensor_copy(posf[:], posi[:]))
            T = [ropet[:, n, :] for n in range(16)]
            for i in range(HALF):
                inv = float(np.float32(THETA ** (-2.0 * i / ROPE)))
                link(v.tensor_scalar(T[4].rearrange("p (t i) -> p t i", i=HALF)[:, :, i], posf[:], inv, None, ALU.mult))
            ang, whole, rem, low, turns, part, cnt = T[4], T[5], T[6], T[7], T[8], T[9], T[10]
            MAGIC = 1.5 * 2.0 ** 23
            TWO_PI = 2.0 * math.pi

            def round_to(dst, src, scale=1.0):
                link(v.tensor_scalar(dst, src, scale, MAGIC, ALU.mult, ALU.add))
                link(v.tensor_scalar(dst, dst, -MAGIC, None, ALU.add))

            def split12(c):
                m, e = math.frexp(c)
                a = math.ldexp(round(m * 2 ** 12), e - 12)
                return a, float(np.float32(c - a))

            round_to(whole, ang, 2.0 ** -20)
            link(v.scalar_tensor_tensor(rem, whole, -2.0 ** 20, ang, ALU.mult, ALU.add))
            round_to(part, rem, 2.0 ** -8)
            link(v.scalar_tensor_tensor(low, part, -2.0 ** 8, rem, ALU.mult, ALU.add))
            first = True
            for count, unit in ((whole, 2.0 ** 20), (part, 2.0 ** 8)):
                frac = unit / TWO_PI
                c_a, c_b = split12(frac - round(frac))
                link(v.tensor_scalar(T[11], count, c_a, None, ALU.mult))
                round_to(cnt, T[11])
                link(v.tensor_tensor(T[11], T[11], cnt, ALU.subtract))
                link(v.scalar_tensor_tensor(T[11], count, c_b, T[11], ALU.mult, ALU.add))
                if first:
                    link(v.tensor_copy(turns, T[11]))
                else:
                    link(v.tensor_tensor(turns, turns, T[11], ALU.add))
                first = False
            round_to(cnt, turns)
            link(v.tensor_tensor(turns, turns, cnt, ALU.subtract))
            pi_a, pi_b = split12(TWO_PI)

            def less_turns(x_):
                round_to(cnt, x_, 1.0 / TWO_PI)
                link(v.scalar_tensor_tensor(x_, cnt, -pi_a, x_, ALU.mult, ALU.add))
                link(v.scalar_tensor_tensor(x_, cnt, -pi_b, x_, ALU.mult, ALU.add))

            less_turns(low)
            link(v.scalar_tensor_tensor(low, turns, TWO_PI, low, ALU.mult, ALU.add))
            LIMIT = 3.1415925
            for n, shift in enumerate((0.0, math.pi / 2)):
                link(v.tensor_scalar(T[n], low, shift, None, ALU.add))
                less_turns(T[n])
            v.tensor_scalar(ropet[:, 0:2, :], ropet[:, 0:2, :], LIMIT, -LIMIT, ALU.min, ALU.max).then_inc(rope_dve, 1)

            lam_sum = [v.tensor_tensor_reduce(out=lam_t[:, n, :], in0=lam_in[:, 2 * n, :], in1=lam_in[:, 2 * n + 1, :],
                                              scale=1.0, scalar=0.0, op0=ALU.mult, op1=ALU.add,
                                              accum_out=lam_e[:, 2 + n:3 + n]) for n in range(2)]
            lam_sum[1].then_inc(lam_exp, 1)

            def input_norm(t):
                dve.wait_ge(sq_done, t + 1)
                v.tensor_scalar(st_v[:, t:t + 1], st_ss[:, t:t + 1], 1.0 / D, EPS, ALU.mult, ALU.add)\
                    .then_inc(v_done, 1)
                dve.wait_ge(r_done, t + 1)
                if t >= 2:
                    dve.wait_ge(hn_turned, 2 * (t - 1))
                v.scalar_tensor_tensor(hn[:, t % 2, :], x_nat[:, t, :], st_r[:, t:t + 1], g_bc[:],
                                       ALU.mult, ALU.mult).then_inc(hn_done, 1)

            def h_lo(n):
                t, half = n // 2, n % 2
                dve.wait_ge(h_hi_done, n + 1)
                dst = slice(4 * half, 4 * half + 4), slice(t * P, (t + 1) * P)
                v.tensor_tensor(hT_lo[:, dst[0], dst[1]], bank[4 + n % 4][:].rearrange("p (c t) -> p c t", c=4),
                                f32(hT_hi[:, dst[0], dst[1]]), ALU.subtract).then_inc(h_lo_done, 1)

            def split_lo(s, k, slot, width=PIECE):
                if isinstance(s, int):
                    dve.wait_ge(w_hi_done, 4 * s + k + 1)
                else:
                    dve.wait_ge(w_hi_done, s * 4 + (k + 1))
                cols = slice(k * width, (k + 1) * width)
                v.tensor_tensor(w_lo[slot][:, cols], raw[k][:, 0:width], f32(w_hi[slot][:, cols]), ALU.subtract)\
                    .then_inc(w_lo_done, 1)

            input_norm(0)
            input_norm(1)
            for t in range(NT):
                h_lo(2 * t)
                h_lo(2 * t + 1)
                if t + 2 < NT:
                    input_norm(t + 2)
                split_lo(0, t, 0)

            dve.wait_ge(rope_act, 1)
            for n in range(2):
                for table, src in ((rope_s[n], T[2]), (rope_c[n], T[3])):
                    sv = src.rearrange("p (t i) -> p t i", i=HALF)
                    for hf in range(2):
                        gb = rope_g[:, n:n + 1, hf * HALF:(hf + 1) * HALF].to_broadcast([P, NT, HALF])
                        link(v.tensor_tensor(table[:, :, hf * HALF:(hf + 1) * HALF], sv, gb, ALU.mult))
            dve.wait_ge(rope_act, 2)
            link(v.tensor_tensor(neg_lam[:], lam_e[:, 1:2], lam_e[:, 0:1], ALU.subtract))
            link(v.tensor_scalar(neg_lam[:], neg_lam[:], -LAMBDA_INIT, None, ALU.add))
            dve.wait_ge(gains_loaded, 16 * 9)
            link(v.tensor_scalar(sub_col[:], sub_col[:], 1.0 - LAMBDA_INIT, None, ALU.mult))
            v.tensor_scalar(qk_col[:, 0:1], qk_col[:, 0:1], 1.0 / math.sqrt(QK), None, ALU.mult)\
                .then_inc(cols_ready, 1)

            def qk_sum(n):
                dve.wait_ge(qk_squared, n + 1)
                if n >= 2:
                    dve.wait_ge(qk_r_done, n - 1)
                link(v.tensor_reduce(qk_ss[:, n % 2, :], qsq[n % 2][:].rearrange("p (g d) -> p g d", d=QK), AX.X, ALU.add))
                v.tensor_scalar(qk_v[:, n % 2, :], qk_ss[:, n % 2, :], 1.0 / QK, EPS, ALU.mult, ALU.add)\
                    .then_inc(qk_v_done, 1)

            def qk_norm(n):
                which, half, t = n // 8, n // 4 % 2, n % 4
                dve.wait_ge(qk_r_done, n + 1)
                full, turn = [P, 4, 2, QK], [P, 4, 2, ROPE]
                r = qk_r[:, n % 2, :].rearrange("p (h m) -> p h m", m=2).unsqueeze(3).to_broadcast(full)
                cos_t = rope_c[which][:, t, :].unsqueeze(1).unsqueeze(1).to_broadcast(turn)
                sin_t = rope_s[which][:, t, :].unsqueeze(1).unsqueeze(1).to_broadcast(turn)
                dst = qkn[:, 4 * half:4 * half + 4, which, t, :].rearrange("p h (m d) -> p h m d", m=2)
                link(v.tensor_tensor(dst, qs[n % 2][:].rearrange("p (h m d) -> p h m d", h=4, m=2), r, ALU.mult))
                rc, rs = (rt[k][:].rearrange("p (h m) d -> p h m d", m=2) for k in range(2))
                link(v.tensor_tensor(rc, dst[:, :, :, 0:ROPE], cos_t, ALU.mult))
                link(v.tensor_tensor(rs, dst[:, :, :, 0:ROPE], sin_t, ALU.mult))
                link(v.tensor_tensor(dst[:, :, :, 0:HALF], rc[:, :, :, 0:HALF], rs[:, :, :, HALF:ROPE], ALU.subtract))
                last = v.tensor_tensor(dst[:, :, :, HALF:ROPE], rc[:, :, :, HALF:ROPE], rs[:, :, :, 0:HALF], ALU.add)
                last.then_inc(qk_ready, 1)

            def v_lo_part(s, t):
                n = NT * s + t
                dve.wait_ge(v_hi_done, n - 15)
                cols = slice((s - 4) * BANK, (s - 3) * BANK)
                v.tensor_tensor(v_lo[:, t, cols], bank[n % 4][:], f32(v_hi[:, t, cols]), ALU.subtract)\
                    .then_inc(v_lo_done, 1)

            for s in range(WO0):
                for t in range(NT):
                    n = NT * s + t
                    if s < 4:
                        qk_sum(n)
                        split_lo(s + 1, t, (s + 1) % 2)
                        qk_norm(n)
                    else:
                        split_lo(s + 1, t, (s + 1) % 2)
                        v_lo_part(s, t)

            def qkT_lo_part(h):
                for n in range(2):
                    dve.wait_ge(qkT_hi_done, 2 * h + n + 1)
                    v.scalar_tensor_tensor(qkT_lo[n][h % 2][:], bank[6 + n][:], qk_col[:, n:n + 1],
                                           f32(qkT_hi[n][h % 2][:]), ALU.mult, ALU.subtract).then_inc(qkT_lo_done, 1)

            qkT_lo_part(0)
            for i in range(NH * NT + 5):
                if i < NH * NT:
                    dve.wait_ge(scored, i + 1)
                    if i >= 2:
                        dve.wait_ge(exp_done, 2 * (i - 1))
                    for m in range(2):
                        last = v.tensor_reduce(nmax[:, i % 2, m:m + 1], bank[2 * (i % 2) + m][:], AX.X, ALU.max,
                                               negate=True)
                    last.then_inc(max_done, 1)
                if 1 <= i <= NH * NT:
                    q = (i - 1) % 2
                    dve.wait_ge(exp_done, 2 * i)
                    link(v.reciprocal(rl[:, q, :], lsum[:, q, :]))
                    v.tensor_copy(rl0[:, i - 1:i], rl[:, q, 0:1])
                    link(v.scalar_tensor_tensor(mixc[:, q, :], lsum[:, q, 0:1], neg_lam[:, 0:1], rl[:, q, 1:2],
                                                ALU.mult, ALU.mult))
                    v.scalar_tensor_tensor(probs[q][:, 0, :], probs[q][:, 1, :], mixc[:, q, :], probs[q][:, 0, :],
                                           ALU.mult, ALU.add).then_inc(a_done, 1)
                if 2 <= i <= NH * NT + 1:
                    t = (i - 2) % NT
                    dve.wait_ge(aT_hi_done, i - 1)
                    v.tensor_tensor(aT_lo[:, :, t * P:(t + 1) * P], bank[4][:].rearrange("p (k t) -> p k t", k=NT),
                                    f32(aT_hi[:, :, t * P:(t + 1) * P]), ALU.subtract).then_inc(aT_lo_done, 1)
                if i % NT == 3 and i // NT + 1 < NH:
                    qkT_lo_part(i // NT + 1)
                if i >= 6 and (i - 6) % NT == 0:
                    h = (i - 6) // NT
                    q = h % 2 * NT
                    mine = rl0[:, NT * h:NT * h + NT]
                    dve.wait_ge(o_summed, h + 1)
                    if h >= 1:
                        dve.wait_ge(o_spread, h)
                    link(v.tensor_tensor(o_v[:, 2 * q + NT:2 * q + 2 * NT], mine, mine, ALU.mult))
                    link(v.tensor_tensor(o_v[:, 2 * q:2 * q + NT], bank[5][:, 0:NT], o_v[:, 2 * q + NT:2 * q + 2 * NT],
                                         ALU.mult))
                    v.tensor_scalar(o_v[:, 2 * q:2 * q + NT], o_v[:, 2 * q:2 * q + NT], 1.0 / VD, EPS,
                                    ALU.mult, ALU.add).then_inc(o_v_done, 1)
                    dve.wait_ge(o_r_done, h + 1)
                    link(v.tensor_tensor(o_v[:, 2 * q + NT:2 * q + 2 * NT], o_r[:, q:q + NT], mine, ALU.mult))
                    v.tensor_tensor(odiag[:], ident[:].unsqueeze(1).to_broadcast([P, NT, P]),
                                    o_v[:, 2 * q + NT:2 * q + 2 * NT].unsqueeze(2).to_broadcast([P, NT, P]),
                                    ALU.mult).then_inc(o_diag_done, 1)
                    dve.wait_ge(o_spread, h + 1)
                    v.tensor_tensor(oc[:], oc[:], bank[5][:], ALU.mult).then_inc(o_normed, 1)
                if i >= 8 and (i - 8) % NT == 0:
                    h = (i - 8) // NT
                    dve.wait_ge(oT_hi_done, h + 1)
                    v.scalar_tensor_tensor(oT[h][:, 1, :], oc[:], sub_col[:, 0:1], f32(oT[h][:, 0, :]),
                                           ALU.mult, ALU.subtract).then_inc(oT_lo_done, 1)

            def add_y(t, c, src):
                dve.wait_ge(y_ready, t + 1)
                if not isinstance(t, int) or t >= NC:
                    dve.wait_ge(y_added, t - (NC - 1))
                v.tensor_tensor(xT[:, c, :], xT[:, c, :], src, ALU.add).then_inc(y_added, 1)

            dve.wait_ge(x_kept, 8)

            def down_phase(s, slot, y0, width=PIECE, last=False):
                for k in range(4):
                    if not last:
                        split_lo(s + 1, k, 1 - slot, width)
                    for c in (2 * k, 2 * k + 1):
                        add_y(y0 + c, c, bank[4 + c % 4][:])

            for s in range(WO0, MLP0):
                down_phase(s, s % 2, NC * (s - WO0))

            def norm_lo(m):
                for c in range(NC):
                    dve.wait_ge(n_hi, NC * m + c + 1)
                    v.scalar_tensor_tensor(hT_lo[:, c, :], xT[:, c, :], gcol[:, m, c:c + 1], f32(hT_hi[:, c, :]),
                                           ALU.mult, ALU.subtract).then_inc(n_lo, 1)

            def norm_v(m):
                dve.wait_ge(n_stat, m + 1)
                v.tensor_scalar(st_v[:, 0:NT], bank[7][:, 0:NT], 1.0 / D, EPS, ALU.mult, ALU.add).then_inc(n_v, 1)

            def norm_diag(m, n):
                dve.wait_ge(n_r, m + 1)
                v.tensor_tensor(z[:, 0, :].rearrange("p (t q) -> p t q", t=NT), ident[:].unsqueeze(1).to_broadcast([P, NT, P]),
                                st_r[:, 0:NT].unsqueeze(2).to_broadcast([P, NT, P]), ALU.mult).then_inc(n_diag, 1)

            def up_phase(s, slot, b, after_split=None):
                if after_split is not None:
                    for f in range(CH):
                        split_lo(s + 1, f, 1 - slot)
                    after_split()
                for f in range(CH):
                    if after_split is None:
                        split_lo(s + 1, f, 1 - slot)
                    dve.wait_ge(h1_ready, b * CH + f + 1)
                    v.scalar_tensor_tensor(z[:, f % 2, :], bank[f][:], 0.0, r_bc[:], ALU.max, ALU.mult)\
                        .then_inc(z_done, 1)
                    dve.wait_ge(zz_done, b * CH + (f + 1))
                    v.tensor_tensor(uT_lo[:, f, :], zz[:, f % 2, :], f32(uT_hi[:, f, :]), ALU.subtract)\
                        .then_inc(u_lo_done, 1)

            for layer in range(2):
                base = MLP_SLAB[layer]
                slot = base % 2
                if layer:
                    norm_lo(1)
                    for k in range(4):
                        split_lo(MLP1, k, MLP1 % 2)
                    norm_v(1)
                    dve.wait_ge(n_r, 2)
                    for gi, w in enumerate(WINDOWS):
                        for t in range(NT):
                            dve.wait_ge(zn_hi_done, NT * gi + (t | 1) + 1)
                            if gi >= 2:
                                dve.wait_ge(pooled, 2 * (gi - 1))
                            v.scalar_tensor_tensor(zn_lo[:, gi % 2, t, :],
                                                   bank[2 * gi + t // 2][:, t % 2 * GW:(t % 2 + 1) * GW],
                                                   st_r[:, t:t + 1], f32(zn_hi[:, gi % 2, t, :]),
                                                   ALU.mult, ALU.subtract).then_inc(zn_lo_done, 1)
                    for c in range(NC):
                        dve.wait_ge(pooled, c + 1)
                        if c >= 2:
                            dve.wait_ge(pool_added, c - 1)
                        if c == 0:
                            dve.wait_ge(band_ready, 1)
                        link(v.scalar_tensor_tensor(zz[:, c % 2, :], bank[c][:], gcol[:, 3, c:c + 1],
                                                    inv_cnt[:, c // 2, :], ALU.mult, ALU.mult))
                        v.tensor_tensor(xT[:, c, :], xT[:, c, :], zz[:, c % 2, :], ALU.add).then_inc(pool_added, 1)
                m = 2 * layer
                norm_lo(m)

                def stats():
                    norm_v(m)
                    norm_diag(m, layer)
                    dve.wait_ge(n_rbc, layer + 1)

                up_phase(base, slot, NB * layer, stats)
                with dve.Fori(0, NB - 1) as j:
                    down_phase(j * 2 + (base + 1), 1 - slot, j * NC + Y_MLP[layer])
                    up_phase(j * 2 + (base + 2), slot, j + (NB * layer + 1))
                down_phase(base + 2 * NB - 1, 1 - slot, Y_MLP[layer] + NC * (NB - 1), 2 * GW, last=layer == 1)

        @block.tensor
        def _(pe):
            def mm(o, lhsT, rhs, start=False, stop=False, **kw):
                return nc.tensor.matmul(o, lhsT, rhs, start=start, stop=stop, **kw)

            def three(o, lh, ll, rh, rl_, start, stop):
                mm(o, lh, rh, start=start)
                mm(o, lh, rl_)
                return mm(o, ll, rh, stop=stop)

            pe.wait_ge(consts, 3)

            def turn_x(t):
                pe.wait_ge(x_loaded[t], 16)
                for half in range(2):
                    n = 2 * t + half
                    if n >= 4:
                        pe.wait_ge(x_kept, n - 3)
                    for c in range(4):
                        last = nc.tensor.transpose(bank[n % 4][:, c * P:(c + 1) * P],
                                                   x_nat[:, t, (4 * half + c) * P:(4 * half + c + 1) * P], ident[:])
                    last.then_inc(x_turned, 1)

            def turn_hn(t):
                pe.wait_ge(hn_done, t + 1)
                for half in range(2):
                    n = 2 * t + half
                    if n >= 4:
                        pe.wait_ge(h_lo_done, n - 3)
                    for c in range(4):
                        last = nc.tensor.transpose(bank[4 + n % 4][:, c * P:(c + 1) * P],
                                                   hn[:, t % 2, (4 * half + c) * P:(4 * half + c + 1) * P], ident[:])
                    last.then_inc(hn_turned, 1)

            turn_x(0)
            turn_x(1)
            turn_hn(0)
            turn_x(2)
            turn_hn(1)
            turn_x(3)
            turn_hn(2)
            turn_hn(3)

            for s in range(WO0):
                hi, lo = w_hi[s % 2], w_lo[s % 2]
                for t in range(NT):
                    n = NT * s + t
                    if n < 4:
                        pe.wait_ge(x_kept, 5 + n)
                    elif n - 4 < 16:
                        pe.wait_ge(qk_copied, n - 3)
                    else:
                        pe.wait_ge(v_lo_done, n - 3 - 16)
                    for c in range(NC):
                        if t == 0 and c % 2 == 0:
                            pe.wait_ge(w_lo_done, 4 * s + c // 2 + 1)
                        if s == 0 and c % 4 == 0:
                            pe.wait_ge(h_lo_done, 2 * t + c // 4 + 1)
                        cols = slice(t * P, (t + 1) * P)
                        last = three(bank[n % 4][:], hT_hi[:, c, cols], hT_lo[:, c, cols],
                                     hi[:, c * BANK:(c + 1) * BANK], lo[:, c * BANK:(c + 1) * BANK],
                                     c == 0, c == NC - 1)
                    last.then_inc(proj_done, 1)

            def turn_qk(h):
                for n in range(2):
                    if h:
                        pe.wait_ge(qkT_lo_done, 2 * h - 1 + n)
                    for t in range(NT):
                        last = nc.tensor.transpose(bank[6 + n][:, t * P:(t + 1) * P], qkn[:, h, n, t, :], ident[:])
                    last.then_inc(qk_turned, 1)

            pe.wait_ge(qk_ready, 16)
            pe.wait_ge(h_lo_done, 8)
            turn_qk(0)
            pe.wait_ge(v_lo_done, 8)
            for i in range(NH * NT + 5):
                if i < NH * NT:
                    h, t = divmod(i, NT)
                    if t == 0:
                        pe.wait_ge(qkT_lo_done, 2 * h + 2)
                    if i >= 2:
                        pe.wait_ge(exp_done, 2 * (i - 1))
                    qh, ql, kh, kl = (y[h % 2] for y in (qkT_hi[0], qkT_lo[0], qkT_hi[1], qkT_lo[1]))
                    cols = slice(t * P, (t + 1) * P)
                    for n, (lhs, rhs) in enumerate(((qh, kh), (qh, kl), (ql, kh))):
                        for m in range(2):
                            rows = slice(m * QK, (m + 1) * QK)
                            last = mm(bank[2 * (i % 2) + m][:], lhs[rows, cols], rhs[rows, :], start=n == 0, stop=n == 2)
                    last.then_inc(scored, 1)
                    if t == 2 and h + 1 < NH:
                        turn_qk(h + 1)
                if i >= 5 and (i - 5) % NT == 0:
                    h = (i - 5) // NT
                    pe.wait_ge(aT_lo_done, NT * h + NT)
                    if h:
                        pe.wait_ge(o_normed, h)
                    cols = slice(h * VD, (h + 1) * VD)
                    for k in range(NT):
                        last = three(bank[5][:], v_hi[:, k, cols], v_lo[:, k, cols], aT_hi[:, k, :], aT_lo[:, k, :],
                                     k == 0, k == NT - 1)
                    last.then_inc(pv_done, 1)
                if 1 <= i <= NH * NT:
                    pe.wait_ge(a_done, i)
                    if i >= 2:
                        pe.wait_ge(aT_lo_done, i - 1)
                    for k in range(NT):
                        last = nc.tensor.transpose(bank[4][:, k * P:(k + 1) * P],
                                                   probs[(i - 1) % 2][:, 0, k * P:(k + 1) * P], ident[:])
                    last.then_inc(a_turned, 1)
                if i >= 5 and (i - 5) % NT == 0:
                    h = (i - 5) // NT
                    pe.wait_ge(o_squared, h + 1)
                    for t in range(NT):
                        last = mm(bank[5][:, t:t + 1], osq[:, t * P:(t + 1) * P], ones[:, 0:1], start=True, stop=True)
                    last.then_inc(o_summed, 1)
                if i >= 6 and (i - 6) % NT == 0:
                    h = (i - 6) // NT
                    pe.wait_ge(o_diag_done, h + 1)
                    mm(bank[5][:], ones[:], odiag[:].rearrange("p t q -> p (t q)"), start=True, stop=True)\
                        .then_inc(o_spread, 1)

            def down(slot, y0, rhs_hi, rhs_lo, first_w, rhs_wait):
                for pair in range(NC // 2):
                    for ks in ((0, 1, 2), (3,)):
                        for c in (2 * pair, 2 * pair + 1):
                            if ks[0] == 0:
                                if not isinstance(y0, int) or y0 + c >= 4:
                                    pe.wait_ge(y_added, y0 + (c - 3))
                            for k in ks:
                                if pair == 0 and c == 0:
                                    pe.wait_ge(w_lo_done, first_w + (k + 1))
                                    rhs_wait(k)
                                cols = slice(k * D + c * P, k * D + (c + 1) * P)
                                last = three(bank[4 + c % 4][:], w_hi[slot][:, cols], w_lo[slot][:, cols],
                                             rhs_hi(k), rhs_lo(k), k == 0, k == 3)
                            if ks[0] == 3:
                                last.then_inc(y_ready, 1)

            def up(slot, b, first_w, between=None, first=False):
                for f in range(CH):
                    if not first:
                        pe.wait_ge(z_done, b * CH + (f - 3))
                    for c in range(NC):
                        if f == 0 and c % 2 == 0:
                            pe.wait_ge(w_lo_done, first_w + (c // 2 + 1))
                        if f == 0 and between is not None:
                            between(c)
                        cols = slice(c * FB + f * P, c * FB + (f + 1) * P)
                        last = three(bank[f][:], w_hi[slot][:, cols], w_lo[slot][:, cols], hT_hi[:, c, :], hT_lo[:, c, :],
                                     c == 0, c == NC - 1)
                    last.then_inc(h1_ready, 1)
                    yield f

            pe.wait_ge(aT_lo_done, NH * NT)
            pe.wait_ge(o_normed, NH)
            pe.wait_ge(qkT_lo_done, 2 * NH)
            for s in range(WO0, MLP0):
                h0 = 4 * (s - WO0)
                down(s % 2, NC * (s - WO0), lambda k: oT[h0 + k][:, 0, :], lambda k: oT[h0 + k][:, 1, :],
                     4 * s, lambda k: pe.wait_ge(oT_lo_done, h0 + k + 1))

            def stat(m):
                pe.wait_ge(n_summed, (NC - 1) * (m + 1))
                for t in range(NT):
                    last = mm(bank[7][:, t:t + 1], nsum[:, t * P:(t + 1) * P], ones[:, 0:1], start=True, stop=True)
                last.then_inc(n_stat, 1)

            def spread(n):
                pe.wait_ge(n_diag, n + 1)
                mm(bank[6][:], ones[:], z[:, 0, :], start=True, stop=True).then_inc(n_spread, 1)

            for layer in range(2):
                base = MLP_SLAB[layer]
                slot = base % 2
                m = 2 * layer
                if layer:
                    ps = POOLS % 2

                    def pool_map(gi, ts):
                        for t in ts:
                            for c in range(2):
                                if t == ts[0] and c == 0:
                                    pe.wait_ge(w_lo_done, 4 * POOLS + gi + 1)
                                if t == 0:
                                    pe.wait_ge(n_lo, NC + 2 * gi + c + 1)
                                cols = slice(t * P, (t + 1) * P)
                                wc = slice((2 * gi + c) * GW, (2 * gi + c + 1) * GW)
                                last = three(bank[2 * gi + t // 2][:, t % 2 * GW:(t % 2 + 1) * GW],
                                             hT_hi[:, 2 * gi + c, cols], hT_lo[:, 2 * gi + c, cols],
                                             w_hi[ps][:, wc], w_lo[ps][:, wc], c == 0, c == 1)
                        return last

                    pe.wait_ge(z_done, NB * CH)
                    pe.wait_ge(y_added, Y_MLP[1])
                    for gi in range(3):
                        pool_map(gi, range(NT)).then_inc(zn_ready, 1)
                    stat(1)
                    pool_map(3, range(2))
                    pe.wait_ge(n_v, 2)
                    pool_map(3, range(2, NT)).then_inc(zn_ready, 1)
                    pe.wait_ge(band_ready, 1)
                    for c in range(NC):
                        gi = c // 2
                        pe.wait_ge(zn_lo_done, NT * (gi + 1))
                        for t in range(NT):
                            b0, b1 = max(t * P - PAD, 0), min(t * P + P + PAD, S)
                            c0 = b0 - (t * P - PAD)
                            rhs = band[:, gi, t, c0:c0 + b1 - b0]
                            zc = slice(c % 2 * P, (c % 2 + 1) * P)
                            mm(bank[c][:, b0:b1], zn_hi[:, gi % 2, t, zc], rhs, start=t == 0, skip_group_check=True)
                            last = mm(bank[c][:, b0:b1], zn_lo[:, gi % 2, t, zc], rhs, stop=t == NT - 1,
                                      skip_group_check=True)
                        last.then_inc(pooled, 1)
                    pe.wait_ge(pool_added, NC)

                def need_h(c, m=m):
                    pe.wait_ge(n_lo, NC * m + c + 1)

                for f in up(slot, NB * layer, 4 * base, need_h, first=True):
                    if f == 1:
                        stat(m)
                    if f == 2:
                        spread(layer)
                with pe.Fori(0, NB - 1) as j:
                    down(1 - slot, j * NC + Y_MLP[layer], lambda k: uT_hi[:, k, :], lambda k: uT_lo[:, k, :],
                         j * 8 + 4 * (base + 1),
                         lambda k: pe.wait_ge(u_lo_done, j * CH + (NB * CH * layer + k + 1)))
                    for _ in up(slot, j + (NB * layer + 1), j * 8 + 4 * (base + 2)):
                        pass
                down(1 - slot, NC * (NB - 1) + Y_MLP[layer], lambda k: uT_hi[:, k, :], lambda k: uT_lo[:, k, :],
                     4 * (base + 2 * NB - 1),
                     lambda k: pe.wait_ge(u_lo_done, CH * (NB - 1) + NB * CH * layer + k + 1))
            pe.wait_ge(z_done, 2 * NB * CH)
            for c in range(NC):
                pe.wait_ge(y_added, Y_MLP[1] + NC * (NB - 1) + c + 1)
                if c >= 4:
                    pe.wait_ge(out_kept, c - 3)
                for t in range(NT):
                    last = nc.tensor.transpose(bank[c % 4][:, t * P:(t + 1) * P], xT[:, c, t * P:(t + 1) * P], ident[:])
                last.then_inc(out_turned, 1)


_INS = ["x", "positions", "norm_mix", "norm_mlp", "attn_w_qkv", "attn_w_o", "attn_q_gain", "attn_k_gain",
        "attn_lam_q1", "attn_lam_k1", "attn_lam_q2", "attn_lam_k2", "attn_sub_gain", "pool_w", "pool_scale",
        "mlp_w1", "mlp_w2"]
_ONE_LAYER = {"attn_w_qkv", "attn_w_o", "attn_q_gain", "attn_k_gain", "attn_lam_q1", "attn_lam_k1",
              "attn_lam_q2", "attn_lam_k2", "attn_sub_gain", "pool_w", "pool_scale"}


def kernel(**inputs):
    import concourse.bacc as bacc
    from concourse.bass_utils import run_bass_kernel_spmd

    nc = bacc.Bacc("TRN2", target_bir_lowering=False, num_devices=1, dynamic_dma_scratch_size=1024)
    arrays, args = {}, []
    for name in _INS:
        a = np.ascontiguousarray(inputs[name])
        arrays[f"in_{name}"] = a
        ap = nc.dram_tensor(f"in_{name}", a.shape, mybir.dt.from_np(a.dtype), kind="ExternalInput").ap()
        args.append(ap[0] if name in _ONE_LAYER else ap)
    args.append(nc.dram_tensor("out", (1, S, D), F32, kind="ExternalOutput").ap())
    build_trunk(nc, *args)
    r = run_bass_kernel_spmd(nc, [arrays], core_ids=[0])
    return r.results[0]["out"]
```

```python
import math
from contextlib import ExitStack

import numpy as np

import concourse.bass as bass
from concourse import mybir

F32 = mybir.dt.float32
F32R = mybir.dt.float32r
I32 = mybir.dt.int32
ALU = mybir.AluOpType
ACT = mybir.ActivationFunctionType
AX = mybir.AxisListType

P = 128
D = 1024
S = 512
DFF = 4096
QK = 64
VD = 128
NH = D // VD
ROPE = QK // 4
HALF = ROPE // 2
THETA = 500000.0
WINDOWS = (2, 4, 8, 16)
NG = len(WINDOWS)
GW = D // NG
EPS = 1e-6
NC = D // P
NT = S // P
BANK = 512
SLAB = 8 * BANK
PIECE = SLAB // 4
FB = 512
NB = DFF // FB
CH = FB // P
LAMBDA_INIT = 0.8 - 0.6 * math.exp(-0.3 * 0)
PAD = max(WINDOWS) // 2
BW = P + 2 * PAD

STEPS = NH * NT
PROJ = ((0, 0), (1, 0), (2, 0), (0, 1), (1, 1), (2, 1))
AHEAD = 3
F_V, F_WO, F_X, F_END = 8, 12, 20, 28


def filler_steps():
    at = {(u // 2, u % 2): u * 13 // 16 for u in range(2 * F_V)}
    at |= {(8, 0): 13, (8, 1): 14, (9, 0): 15, (9, 1): 16, (10, 0): 19, (10, 1): 19, (11, 0): 20, (11, 1): 21}
    at |= {(F_WO + k, u): (22, 23, 25, 26, 27, 29, 30, 31)[k] for k in range(NC) for u in range(2)}
    at |= {(F_X + k, u): STEPS + 1 + k // 2 for k in range(NC) for u in range(2)}
    return at


FILL = filler_steps()
TAKE = {f: FILL[f, 1] + 1 for f in range(F_V)} | {8: 18, 9: 19, 10: 20, 11: 22}
SPLIT = {4: (0, 1, 3, 4), 5: (6, 8, 10, 12), 6: (14, 16, 18, 20), 7: (23, 25, 27, 29)}
LAST = STEPS + 7

WO0 = 6
MLP0 = WO0 + 2
POOLS = MLP0 + 2 * NB
MLP1 = POOLS + 1
NSLAB = MLP1 + 2 * NB
MLP_SLAB = (MLP0, MLP1)
Y_MLP = (16, 16 + 8 * NB)


def build_trunk(nc, x, positions, norm_mix, norm_mlp, w_qkv, w_o, q_gain, k_gain, lam_q1, lam_k1,
                lam_q2, lam_k2, sub_gain, pool_w, pool_scale, w1, w2, out):
    ctx = ExitStack()
    with ctx:
        cursor = [-(-nc.sbuf_base // 32) * 32]

        def at(name, shape, dt, offset):
            return nc.alloc_sbuf_tensor_at("s_" + name, shape, dt, offset=offset)

        def size(shape):
            n = 4
            for k in shape[1:]:
                n *= k
            return -(-n // 32) * 32

        def sb(name, shape, dt=F32):
            t = at(name, shape, dt, cursor[0])
            cursor[0] += size(shape)
            return t

        def region(kbytes):
            base = cursor[0]
            cursor[0] += kbytes * 1024
            return base

        def inside(base, *wanted):
            made = []
            for name, shape, dt in wanted:
                made.append(at(name, shape, dt, base))
                base += size(shape)
            return made

        def sem(name):
            return ctx.enter_context(nc.semaphore(name))

        raw = [sb(f"raw{k}", [P, PIECE]) for k in range(4)]
        w_hi = [sb(f"w_hi{k}", [P, SLAB], F32R) for k in range(2)]
        w_lo = [sb(f"w_lo{k}", [P, SLAB], F32R) for k in range(2)]
        x_region = region(16)
        (xT,) = inside(x_region, ("xT", [P, NC, S], F32))
        h_region = region(32)
        qk_region = region(32)
        v_region = region(16)
        scratch = region(34)
        qkT_hi = [sb(f"{n}T_hi", [P, S], F32R) for n in "qk"]
        qkT_lo = [sb(f"{n}T_lo", [P, S], F32R) for n in "qk"]

        hT_hi, hT_lo = inside(h_region, ("hT_hi", [P, NC, S], F32R), ("hT_lo", [P, NC, S], F32R))
        (x_again,) = inside(h_region, ("x_again", [P, NT, D], F32))
        (qkn,) = inside(qk_region, ("qkn", [P, NH, 2, NT, P], F32))
        oT = inside(qk_region, *[(f"oT{h}", [P, 2, S], F32R) for h in range(NH)])
        uT_hi, uT_lo, z, zz, r_bc, nsum, nsq = inside(
            qk_region, ("uT_hi", [P, CH, S], F32R), ("uT_lo", [P, CH, S], F32R),
            ("z", [P, 2, S], F32), ("zz", [P, 2, S], F32), ("r_bc", [P, S], F32),
            ("nsum", [P, S], F32), ("nsq", [P, 2, S], F32))
        zn_hi, zn_lo = inside(qk_region, ("zn_hi", [P, 2, NT, GW], F32R), ("zn_lo", [P, 2, NT, GW], F32R))
        (onat,) = inside(qk_region, ("onat", [P, 4, NT, P], F32))
        v_hi, v_lo = inside(v_region, ("v_hi", [P, NT, BANK], F32R), ("v_lo", [P, NT, BANK], F32R))
        (x_nat,) = inside(v_region, ("x_nat", [P, NT, D], F32))
        aT_hi, aT_lo, p0, p1, a_raw, oc, osq, odiag = inside(
            scratch, ("aT_hi", [P, NT, S], F32R), ("aT_lo", [P, NT, S], F32R),
            ("p0", [P, 2, S], F32), ("p1", [P, 2, S], F32), ("a_raw", [P, 2, S], F32),
            ("oc", [P, S], F32), ("osq", [P, S], F32), ("odiag", [P, NT, P], F32))
        probs = [p0, p1]
        hn, g_bc, lam_in, lam_t, ropet = inside(
            scratch, ("hn", [P, 2, D], F32), ("g_bc", [P, D], F32),
            ("lam_in", [P, 4, QK], F32), ("lam_t", [P, 2, QK], F32), ("ropet", [P, 16, NT * HALF], F32))
        band_f, band, inv_cnt = inside(
            scratch, ("band_f", [P, NG, NT, BW], F32), ("band", [P, NG, NT, BW], F32R),
            ("inv_cnt", [P, NG, S], F32))
        qs0, qs1, qsq0, qsq1, rt0, rt1 = inside(
            x_region, ("qs0", [P, S], F32), ("qs1", [P, S], F32), ("qsq0", [P, S], F32), ("qsq1", [P, S], F32),
            ("rt0", [P, 2 * NT, ROPE], F32), ("rt1", [P, 2 * NT, ROPE], F32))
        qs, qsq, rt = [qs0, qs1], [qsq0, qsq1], [rt0, rt1]

        ident = sb("ident", [P, P])
        ones = sb("ones", [P, P])
        rope_c = [sb(f"rope_c{n}", [P, NT, ROPE]) for n in "qk"]
        rope_s = [sb(f"rope_s{n}", [P, NT, ROPE]) for n in "qk"]
        minus_half = sb("minus_half", [P, 8])
        gcol = sb("gcol", [P, 4, NC])
        qk_col = sb("qk_col", [P, 2])
        sub_col = sb("sub_col", [P, 1])
        neg_lam = sb("neg_lam", [P, 1])
        lam_e = sb("lam_e", [P, 4])
        st_ss = sb("st_ss", [P, 8])
        st_v = sb("st_v", [P, 8])
        st_r = sb("st_r", [P, 8])
        qk_ss = sb("qk_ss", [P, 2, 8])
        qk_v = sb("qk_v", [P, 2, 8])
        qk_r = sb("qk_r", [P, 2, 8])
        nmax = sb("nmax", [P, 2, 2])
        lsum = sb("lsum", [P, 2, 2])
        rl = sb("rl", [P, 2, 2])
        mixc = sb("mixc", [P, 2, 1])
        rl0 = sb("rl0", [P, NH * NT])
        o_sq = sb("o_sq", [P, NT])
        o_v = sb("o_v", [P, NT])
        o_r = sb("o_r", [P, NT])
        o_rl = sb("o_rl", [P, NT])
        posi = sb("posi", [P, NT], I32)
        posf = sb("posf", [P, NT])
        rope_g = sb("rope_g", [P, 2, ROPE])
        assert cursor[0] <= nc.sbuf_usable_end, (cursor[0], nc.sbuf_usable_end)

        bank = [ctx.enter_context(nc.psum_tensor(f"bank{k}", [P, BANK], F32)) for k in range(8)]

        x_loaded = [sem(f"x_loaded{k}") for k in range(NT)]
        small_loaded = sem("small_loaded")
        rope_loaded = sem("rope_loaded")
        gains_loaded = sem("gains_loaded")
        raw_loaded = [sem(f"raw_loaded{k}") for k in range(4)]
        stored = [sem(f"stored{k}") for k in range(4)]
        w_hi_done = sem("w_hi_done")
        w_lo_done = sem("w_lo_done")
        consts = sem("consts")
        cols_filled = sem("cols_filled")
        cols_ready = sem("cols_ready")
        sq_done = sem("sq_done")
        v_done = sem("v_done")
        r_done = sem("r_done")
        hn_done = sem("hn_done")
        x_turned = sem("x_turned")
        x_added = sem("x_added")
        x_again_loaded = [sem(f"x_again_loaded{k}") for k in range(NT)]
        aT_copied = sem("aT_copied")
        hn_turned = sem("hn_turned")
        h_hi_done = sem("h_hi_done")
        h_lo_done = sem("h_lo_done")
        proj_done = sem("proj_done")
        qk_copied = sem("qk_copied")
        qk_squared = sem("qk_squared")
        qk_v_done = sem("qk_v_done")
        qk_r_done = sem("qk_r_done")
        qk_ready = sem("qk_ready")
        v_hi_done = sem("v_hi_done")
        v_lo_done = sem("v_lo_done")
        rope_dve = sem("rope_dve")
        rope_act = sem("rope_act")
        lam_exp = sem("lam_exp")
        qk_turned = sem("qk_turned")
        qkT_hi_done = sem("qkT_hi_done")
        qkT_lo_done = sem("qkT_lo_done")
        scored = sem("scored")
        max_done = sem("max_done")
        exp_done = sem("exp_done")
        a_done = sem("a_done")
        a_turned = sem("a_turned")
        aT_hi_done = sem("aT_hi_done")
        aT_lo_done = sem("aT_lo_done")
        pv_done = sem("pv_done")
        o_copied = sem("o_copied")
        o_squared = sem("o_squared")
        o_summed = sem("o_summed")
        o_v_done = sem("o_v_done")
        o_r_done = sem("o_r_done")
        o_diag_done = sem("o_diag_done")
        o_spread = sem("o_spread")
        o_normed = sem("o_normed")
        oT_hi_done = sem("oT_hi_done")
        oT_lo_done = sem("oT_lo_done")
        y_ready = sem("y_ready")
        y_added = sem("y_added")
        n_hi = sem("n_hi")
        n_lo = sem("n_lo")
        n_squared = sem("n_squared")
        n_summed = sem("n_summed")
        n_stat = sem("n_stat")
        n_v = sem("n_v")
        n_r = sem("n_r")
        n_diag = sem("n_diag")
        n_spread = sem("n_spread")
        n_rbc = sem("n_rbc")
        h1_ready = sem("h1_ready")
        z_done = sem("z_done")
        u_hi_done = sem("u_hi_done")
        zz_done = sem("zz_done")
        u_lo_done = sem("u_lo_done")
        zn_ready = sem("zn_ready")
        zn_hi_done = sem("zn_hi_done")
        zn_lo_done = sem("zn_lo_done")
        band_ready = sem("band_ready")
        pooled = sem("pooled")
        pool_added = sem("pool_added")
        out_turned = sem("out_turned")
        out_kept = sem("out_kept")
        dve_chain = sem("dve_chain")
        pool_chain = sem("pool_chain")

        def wait_used(eng, s):
            if s < 0:
                return
            if s < WO0:
                eng.wait_ge(proj_done, NT * (s + 1))
            elif s < MLP0:
                eng.wait_ge(y_ready, NC * (s - WO0 + 1))
            elif s == POOLS:
                eng.wait_ge(zn_ready, NG)
            else:
                layer = int(s > POOLS)
                j, down = divmod(s - MLP_SLAB[layer], 2)
                if down:
                    eng.wait_ge(y_ready, Y_MLP[layer] + NC * (j + 1))
                else:
                    eng.wait_ge(h1_ready, CH * (NB * layer + j + 1))

        def f32(ap):
            return ap.bitcast(F32)

        def piece(slab, k):
            if slab < WO0:
                n0 = PROJ[slab][0] * D + PROJ[slab][1] * BANK
                return w_qkv.rearrange("(c p) n -> p c n", p=P)[:, 2 * k:2 * k + 2, n0:n0 + BANK]
            if slab < MLP0:
                return w_o.rearrange("(c p) n -> p c n", p=P)[:, 4 * (slab - WO0) + k, :]
            assert slab == POOLS
            return pool_w[k].rearrange("(c p) n -> p c n", p=P)

        def w1_piece(layer, j, k):
            return w1[layer].rearrange("(c p) n -> p c n", p=P)[:, 2 * k:2 * k + 2, bass.ds(j * FB, FB)]

        def w2_piece(layer, j, k):
            return w2[layer].rearrange("(b k p) n -> p k b n", p=P, k=CH)[:, k, bass.ds(j, 1), :]

        block = ctx.enter_context(nc.Block())

        @block.sync
        def _(sp):
            xv = x.rearrange("a (t p) d -> p (a t) d", p=P)
            for t in range(NT):
                sp.dma_start(x_nat[:, t, :], xv[:, t, :]).then_inc(x_loaded[t], 16)

            def load(slab, k, src, width=PIECE):
                if not isinstance(slab, int) or slab >= 1:
                    sp.wait_ge(w_lo_done, slab * 4 + (k - 3))
                dst = raw[k][:, 0:width]
                if len(src.shape) == 3:
                    dst = dst.rearrange("p (a b) -> p a b", a=src.shape[1])
                sp.dma_start(dst, src).then_inc(raw_loaded[k], 16)

            for s in range(MLP0):
                for k in range(4):
                    load(s, k, piece(s, k))
            wait_used(sp, WO0 - 1)
            for t in range(NT):
                sp.dma_start(x_again[:, t, :], xv[:, t, :]).then_inc(x_again_loaded[t], 16)
            for layer in range(2):
                base = MLP_SLAB[layer]
                if layer:
                    for k in range(4):
                        load(POOLS, k, piece(POOLS, k), 2 * GW)
                for k in range(4):
                    load(base, k, w1_piece(layer, 0, k))
                with sp.Fori(0, NB - 1) as j:
                    for k in range(4):
                        load(j * 2 + (base + 1), k, w2_piece(layer, j, k))
                    for k in range(4):
                        load(j * 2 + (base + 2), k, w1_piece(layer, j + 1, k))
                for k in range(4):
                    load(base + 2 * NB - 1, k, w2_piece(layer, NB - 1, k))
            ov = out.rearrange("a (t p) d -> p (a t) d", p=P)
            for c in range(NC):
                sp.wait_ge(out_kept, c + 1)
                sp.dma_start(ov[:, :, c * P:(c + 1) * P], onat[:, c % 4, :, :]).then_inc(stored[c % 4], 16)
            for k in range(4):
                sp.wait_ge(stored[k], 16 * (NC // 4))

        @block.gpsimd
        def _(pool):
            g = nc.gpsimd
            links = [0]

            def link(ins):
                links[0] += 1
                ins.then_inc(pool_chain, 1)
                pool.wait_ge(pool_chain, links[0])

            g.memset(minus_half[:], -0.5).then_inc(consts, 1)
            g.memset(ones[:], 1.0).then_inc(consts, 1)
            link(g.memset(ident[:], 0.0))
            g.affine_select(out=ident[:], in_=ident[:], compare_op=ALU.not_equal, fill=1.0, base=0,
                            pattern=[[-1, P]], channel_multiplier=1).then_inc(consts, 1)
            pool.wait_ge(consts, 1)

            for t in range(NT):
                pool.wait_ge(v_done, t + 1)
                g.tensor_tensor(st_r[:, t:t + 1], st_v[:, t:t + 1], minus_half[:, 0:1], ALU.pow)\
                    .then_inc(r_done, 1)
            def qk_root(n):
                pool.wait_ge(qk_copied, n + 1)
                if n >= 2:
                    pool.wait_ge(qk_v_done, n - 1)
                g.tensor_tensor(qsq[n % 2][:], qs[n % 2][:], qs[n % 2][:], ALU.mult).then_inc(qk_squared, 1)
                pool.wait_ge(qk_v_done, n + 1)
                if n >= 2:
                    pool.wait_ge(qk_ready, n - 1)
                g.tensor_tensor(qk_r[:, n % 2, :], qk_v[:, n % 2, :], minus_half[:], ALU.pow)\
                    .then_inc(qk_r_done, 1)

            for n in range(2 * NT):
                qk_root(n)
            for i in range(LAST):
                if 2 <= i < STEPS + 2:
                    t = (i - 2) % NT
                    pool.wait_ge(aT_copied, i - 1)
                    g.tensor_tensor(aT_lo[:, :, t * P:(t + 1) * P], a_raw[:, i % 2, :].rearrange("p (k t) -> p k t", k=NT),
                                    f32(aT_hi[:, :, t * P:(t + 1) * P]), ALU.subtract).then_inc(aT_lo_done, 1)
                for f in range(F_V):
                    if TAKE[f] == i:
                        qk_root(2 * NT + f)
                if i >= 7 and (i - 7) % NT == 0:
                    h = (i - 7) // NT
                    pool.wait_ge(o_v_done, h + 1)
                    link(g.tensor_tensor(o_r[:], o_v[:], minus_half[:, 0:NT], ALU.pow))
                    link(g.tensor_tensor(o_rl[:], o_r[:], rl0[:, NT * h:NT * h + NT], ALU.mult))
                    if h:
                        pool.wait_ge(o_spread, h)
                    g.tensor_tensor(odiag[:], ident[:].unsqueeze(1).to_broadcast([P, NT, P]),
                                    o_rl[:].unsqueeze(2).to_broadcast([P, NT, P]), ALU.mult).then_inc(o_diag_done, 1)

            def norm(m):
                for c in range(NC):
                    pool.wait_ge(n_squared, NC * m + c + 1)
                    if c == 0:
                        if m:
                            pool.wait_ge(n_stat, m)
                        continue
                    first = nsq[:, 0, :] if c == 1 else nsum[:]
                    if c >= 2:
                        pool.wait_ge(n_summed, (NC - 1) * m + c - 1)
                    g.tensor_tensor(nsum[:], first, nsq[:, c % 2, :], ALU.add).then_inc(n_summed, 1)
                pool.wait_ge(n_v, m + 1)
                g.tensor_tensor(st_r[:, 0:NT], st_v[:, 0:NT], minus_half[:, 0:NT], ALU.pow).then_inc(n_r, 1)

            norm(0)
            for gi, w in enumerate(WINDOWS):
                hw = w // 2
                v = band_f[:, gi, :, :]
                link(g.memset(v, 1.0))
                link(g.affine_select(out=v, in_=v, compare_op=ALU.is_ge, fill=0.0, base=PAD + hw,
                                     pattern=[[0, NT], [-1, BW]], channel_multiplier=1))
                link(g.affine_select(out=v, in_=v, compare_op=ALU.is_gt, fill=0.0, base=hw - PAD,
                                     pattern=[[0, NT], [1, BW]], channel_multiplier=-1))
                link(g.affine_select(out=v, in_=v, compare_op=ALU.not_equal, fill=float(1 - w), base=PAD,
                                     pattern=[[0, NT], [-1, BW]], channel_multiplier=1))
                link(g.memset(inv_cnt[:, gi, :], 1.0 / w))
                for t in [*range(hw), *range(S - hw + 1, S)]:
                    cnt = min(t + hw, S) - max(t - hw, 0)
                    tile, col = t // P, t % P + PAD
                    one = band_f[:, gi, tile, col:col + 1]
                    g.affine_select(out=one, in_=one, compare_op=ALU.not_equal, fill=float(1 - cnt),
                                    base=-(t % P), pattern=[[0, 1]], channel_multiplier=1)
                    link(g.memset(inv_cnt[:, gi, t:t + 1], float(np.float32(1.0) / np.float32(cnt))))
            g.tensor_copy(band[:], band_f[:]).then_inc(band_ready, 1)
            norm(1)
            norm(2)

        @block.scalar
        def _(act):
            a = nc.scalar
            act.dma_start(g_bc[:], norm_mix[0].partition_broadcast(P)).then_inc(small_loaded, 16)

            def split_hi(s, k, slot, width=PIECE, free=None):
                act.wait_ge(raw_loaded[k], s * 16 + 16)
                if free is not None:
                    free()
                else:
                    wait_used(act, s - 2)
                a.activation(w_hi[slot][:, k * width:(k + 1) * width], raw[k][:, 0:width], ACT.Copy)\
                    .then_inc(w_hi_done, 1)

            def input_squares(t):
                act.wait_ge(x_loaded[t], 16)
                if t >= 2:
                    act.wait_ge(hn_turned, 2 * (t - 1))
                a.activation(hn[:, t % 2, :], x_nat[:, t, :], ACT.Square, accum_out=st_ss[:, t:t + 1])\
                    .then_inc(sq_done, 1)

            def h_hi(n):
                t, half = n // 2, n % 2
                act.wait_ge(hn_turned, n + 1)
                a.activation(hT_hi[:, 4 * half:4 * half + 4, t * P:(t + 1) * P],
                             bank[4 + n % 4][:].rearrange("p (c t) -> p c t", c=4), ACT.Copy)\
                    .then_inc(h_hi_done, 1)

            input_squares(0)
            input_squares(1)
            with nc.allow_non_contiguous_dma("positions and gains as columns, a few KB"):
                act.dma_start(posi[:], positions.rearrange("a (t p) -> p (a t)", p=P)).then_inc(rope_loaded, 16)
                for n, gain in enumerate((q_gain, k_gain)):
                    act.dma_start(rope_g[:, n, :], gain[0:ROPE].partition_broadcast(P)).then_inc(rope_loaded, 16)
                for n, lam in enumerate((lam_q1, lam_k1, lam_q2, lam_k2)):
                    act.dma_start(lam_in[:, n, :], lam.partition_broadcast(P)).then_inc(rope_loaded, 16)
            for t in range(NT):
                h_hi(2 * t)
                h_hi(2 * t + 1)
                if t + 2 < NT:
                    input_squares(t + 2)
                split_hi(0, t, 0)
            act.wait_ge(rope_dve, 1)
            a.activation(ropet[:, 2:4, :], ropet[:, 0:2, :], ACT.Sin).then_inc(rope_act, 1)
            act.wait_ge(lam_exp, 1)
            a.activation(lam_e[:, 0:2], lam_e[:, 2:4], ACT.Exp).then_inc(rope_act, 1)
            with nc.allow_non_contiguous_dma("gains as columns, a few KB"):
                act.wait_ge(cols_filled, 1)
                for n, gain in enumerate((q_gain, k_gain)):
                    for m in range(2):
                        act.dma_start(qk_col[m * QK + ROPE:(m + 1) * QK, n:n + 1],
                                      gain[ROPE:QK].rearrange("(p a) -> p a", a=1)).then_inc(gains_loaded, 16)
                act.dma_start(sub_col[:], sub_gain.rearrange("(p a) -> p a", a=1)).then_inc(gains_loaded, 16)
                for n, col in enumerate((norm_mlp[0], norm_mix[1], norm_mlp[1], pool_scale)):
                    act.dma_start(gcol[:, n, :], col.rearrange("(c p) -> p c", p=P)).then_inc(gains_loaded, 16)

            def qk_copy(n, src, tile):
                act.wait_ge(proj_done, tile + 1)
                if n >= 2:
                    act.wait_ge(qk_ready, n - 1)
                a.activation(qs[n % 2][:], src[:], ACT.Copy).then_inc(qk_copied, 1)

            def v_hi_part(t, src, tile):
                act.wait_ge(proj_done, tile + 1)
                a.activation(v_hi[:, t, :], src[:], ACT.Copy).then_inc(v_hi_done, 1)

            for s in range(AHEAD):
                for t in range(NT):
                    split_hi(s + 1, t, (s + 1) % 2)
                    tile = NT * s + t
                    if PROJ[s][0] < 2:
                        qk_copy(tile, bank[tile % 4], tile)
                    else:
                        v_hi_part(t, bank[tile % 4], tile)

            def qkT(h):
                for n in range(2):
                    act.wait_ge(qk_turned, 2 * h + n + 1)
                    act.wait_ge(scored, NT * h) if h else None
                    a.activation(qkT_hi[n][:], bank[n][:], ACT.Copy, scale=qk_col[:, n:n + 1])\
                        .then_inc(qkT_hi_done, 1)

            def map_part(i):
                h, t = divmod(i, NT)
                act.wait_ge(a_turned, i + 1)
                if t == 0 and h:
                    act.wait_ge(pv_done, h)
                src = bank[4][:].rearrange("p (k t) -> p k t", k=NT)
                a.activation(aT_hi[:, :, t * P:(t + 1) * P], src, ACT.Copy).then_inc(aT_hi_done, 1)
                if i >= 2:
                    act.wait_ge(aT_lo_done, i - 1)
                a.activation(a_raw[:, i % 2, :], bank[4][:], ACT.Copy).then_inc(aT_copied, 1)

            def exps(i):
                act.wait_ge(max_done, i + 1)
                if i >= 2:
                    act.wait_ge(a_turned, i - 1)
                for m in range(2):
                    a.activation(probs[i % 2][:, m, :], bank[2 * (i % 2) + m][:], ACT.Exp,
                                 bias=nmax[:, i % 2, m:m + 1],
                                 accum_out=lsum[:, i % 2, m:m + 1]).then_inc(exp_done, 1)

            act.wait_ge(cols_ready, 1)
            for i in range(LAST):
                if i == TAKE[11]:
                    v_hi_part(3, bank[7], NT * AHEAD + 11)
                late = (i - 2) % NT == 0
                if 2 <= i < STEPS + 2 and not late:
                    map_part(i - 2)
                if i < STEPS:
                    if i % NT == 0:
                        qkT(i // NT)
                    exps(i)
                if 2 <= i < STEPS + 2 and late:
                    map_part(i - 2)
                if i >= 6 and (i - 6) % NT == 0 and (i - 6) // NT < NH:
                    h = (i - 6) // NT
                    act.wait_ge(pv_done, h + 1)
                    if h:
                        act.wait_ge(oT_lo_done, h)
                        act.wait_ge(o_summed, h)
                    a.activation(oc[:], bank[5][:], ACT.Copy).then_inc(o_copied, 1)
                    a.activation(osq[:], bank[5][:], ACT.Square).then_inc(o_squared, 1)
                if i >= 9 and (i - 9) % NT == 0 and (i - 9) // NT < NH:
                    h = (i - 9) // NT
                    act.wait_ge(o_normed, h + 1)
                    a.activation(oT[h][:, 0, :], oc[:], ACT.Copy, scale=sub_col[:, 0:1]).then_inc(oT_hi_done, 1)
                for s, steps in SPLIT.items():
                    for k in range(4):
                        if steps[k] == i:
                            split_hi(s, k, s % 2)
                for f in range(F_V):
                    if TAKE[f] == i:
                        qk_copy(2 * NT + f, bank[6 + f % 2], NT * AHEAD + f)
                for f in (8, 9, 10):
                    if TAKE[f] == i:
                        act.wait_ge(pv_done, 4)
                        v_hi_part(f - 8, bank[6 + f % 2], NT * AHEAD + f)
                for c in range(NC):
                    if FILL[F_WO + c, 1] == i:
                        act.wait_ge(y_ready, c + 1)
                        if c == 0:
                            act.wait_ge(qk_ready, 16)
                        a.activation(xT[:, c, :], bank[6 + c % 2][:], ACT.Copy).then_inc(y_added, 1)

            for k in range(4):
                split_hi(MLP0, k, MLP0 % 2)

            def norm(m, before):
                done, count = before
                if m == 0:
                    act.wait_ge(x_added, NC)
                for c in range(NC):
                    act.wait_ge(done, count - NC + c + 1)
                    a.activation(hT_hi[:, c, :], xT[:, c, :], ACT.Copy, scale=gcol[:, m, c:c + 1])\
                        .then_inc(n_hi, 1)
                for c in range(NC):
                    if m or c >= 2:
                        act.wait_ge(n_summed, (NC - 1) * m + (max(1, c - 2) if c >= 2 else 0))
                    a.activation(nsq[:, c % 2, :], xT[:, c, :], ACT.Square).then_inc(n_squared, 1)

            def spread_copy(m):
                act.wait_ge(n_spread, m + 1)
                a.activation(r_bc[:], bank[6][:], ACT.Copy).then_inc(n_rbc, 1)

            def up_phase(s, slot, b, after_split=None):
                def split(f):
                    split_hi(s + 1, f, 1 - slot, free=lambda: act.wait_ge(y_ready, b * NC + Y_MLP[0]))

                if after_split is not None:
                    for f in range(CH):
                        split(f)
                    after_split()
                for f in range(CH):
                    if after_split is None:
                        split(f)
                    act.wait_ge(z_done, b * CH + (f + 1))
                    a.activation(uT_hi[:, f, :], z[:, f % 2, :], ACT.Square).then_inc(u_hi_done, 1)
                    a.activation(zz[:, f % 2, :], z[:, f % 2, :], ACT.Square).then_inc(zz_done, 1)

            def down_phase(s, slot, b, width=PIECE):
                for k in range(4):
                    split_hi(s + 1, k, 1 - slot, width, free=lambda: act.wait_ge(h1_ready, b * CH + CH))

            for layer in range(2):
                base = MLP_SLAB[layer]
                slot = base % 2
                if layer == 0:
                    norm(0, (y_added, 16))
                else:
                    norm(1, (y_added, Y_MLP[1]))
                    for k in range(4):
                        split_hi(MLP1, k, MLP1 % 2)
                    act.wait_ge(n_r, 2)
                    for gi in range(NG):
                        act.wait_ge(zn_ready, gi + 1)
                        if gi >= 2:
                            act.wait_ge(pooled, 2 * (gi - 1))
                        for t in range(NT):
                            a.activation(zn_hi[:, gi % 2, t, :], bank[2 * gi + t // 2][:, t % 2 * GW:(t % 2 + 1) * GW],
                                         ACT.Copy, scale=st_r[:, t:t + 1]).then_inc(zn_hi_done, 1)
                    norm(2, (pool_added, NC))
                up_phase(base, slot, NB * layer, lambda: spread_copy(layer))
                with act.Fori(0, NB - 1) as j:
                    down_phase(j * 2 + (base + 1), 1 - slot, j + NB * layer)
                    up_phase(j * 2 + (base + 2), slot, j + (NB * layer + 1))
                if layer == 0:
                    down_phase(base + 2 * NB - 1, 1 - slot, NB - 1, 2 * GW)
            for c in range(NC):
                act.wait_ge(out_turned, c + 1)
                if c >= 4:
                    act.wait_ge(stored[c % 4], 16 * (c // 4))
                a.activation(onat[:, c % 4, :, :], bank[c % 4][:].rearrange("p (t c) -> p t c", t=NT), ACT.Copy)\
                    .then_inc(out_kept, 1)

        @block.vector
        def _(dve):
            v = nc.vector
            links = [0]

            def link(ins):
                links[0] += 1
                ins.then_inc(dve_chain, 1)
                dve.wait_ge(dve_chain, links[0])

            v.memset(qk_col[:], 1.0).then_inc(cols_filled, 1)

            def input_norm(t):
                dve.wait_ge(sq_done, t + 1)
                v.tensor_scalar(st_v[:, t:t + 1], st_ss[:, t:t + 1], 1.0 / D, EPS, ALU.mult, ALU.add)\
                    .then_inc(v_done, 1)
                dve.wait_ge(r_done, t + 1)
                if t >= 2:
                    dve.wait_ge(hn_turned, 2 * (t - 1))
                v.scalar_tensor_tensor(hn[:, t % 2, :], x_nat[:, t, :], st_r[:, t:t + 1], g_bc[:],
                                       ALU.mult, ALU.mult).then_inc(hn_done, 1)

            def h_lo(n):
                t, half = n // 2, n % 2
                dve.wait_ge(h_hi_done, n + 1)
                dst = slice(4 * half, 4 * half + 4), slice(t * P, (t + 1) * P)
                v.tensor_tensor(hT_lo[:, dst[0], dst[1]], bank[4 + n % 4][:].rearrange("p (c t) -> p c t", c=4),
                                f32(hT_hi[:, dst[0], dst[1]]), ALU.subtract).then_inc(h_lo_done, 1)

            def split_lo(s, k, slot, width=PIECE):
                if isinstance(s, int):
                    dve.wait_ge(w_hi_done, 4 * s + k + 1)
                else:
                    dve.wait_ge(w_hi_done, s * 4 + (k + 1))
                cols = slice(k * width, (k + 1) * width)
                v.tensor_tensor(w_lo[slot][:, cols], raw[k][:, 0:width], f32(w_hi[slot][:, cols]), ALU.subtract)\
                    .then_inc(w_lo_done, 1)

            dve.wait_ge(small_loaded, 16)
            input_norm(0)
            input_norm(1)
            for t in range(NT):
                h_lo(2 * t)
                h_lo(2 * t + 1)
                if t + 2 < NT:
                    input_norm(t + 2)
                split_lo(0, t, 0)

            dve.wait_ge(rope_loaded, 16 * 7)
            link(v.tensor_copy(posf[:], posi[:]))
            T = [ropet[:, n, :] for n in range(16)]
            for i in range(HALF):
                inv = float(np.float32(THETA ** (-2.0 * i / ROPE)))
                link(v.tensor_scalar(T[4].rearrange("p (t i) -> p t i", i=HALF)[:, :, i], posf[:], inv, None, ALU.mult))
            ang, whole, rem, low, turns, part, cnt = T[4], T[5], T[6], T[7], T[8], T[9], T[10]
            MAGIC = 1.5 * 2.0 ** 23
            TWO_PI = 2.0 * math.pi

            def round_to(dst, src, scale=1.0):
                link(v.tensor_scalar(dst, src, scale, MAGIC, ALU.mult, ALU.add))
                link(v.tensor_scalar(dst, dst, -MAGIC, None, ALU.add))

            def split12(c):
                m, e = math.frexp(c)
                a = math.ldexp(round(m * 2 ** 12), e - 12)
                return a, float(np.float32(c - a))

            round_to(whole, ang, 2.0 ** -20)
            link(v.scalar_tensor_tensor(rem, whole, -2.0 ** 20, ang, ALU.mult, ALU.add))
            round_to(part, rem, 2.0 ** -8)
            link(v.scalar_tensor_tensor(low, part, -2.0 ** 8, rem, ALU.mult, ALU.add))
            first = True
            for count, unit in ((whole, 2.0 ** 20), (part, 2.0 ** 8)):
                frac = unit / TWO_PI
                c_a, c_b = split12(frac - round(frac))
                link(v.tensor_scalar(T[11], count, c_a, None, ALU.mult))
                round_to(cnt, T[11])
                link(v.tensor_tensor(T[11], T[11], cnt, ALU.subtract))
                link(v.scalar_tensor_tensor(T[11], count, c_b, T[11], ALU.mult, ALU.add))
                if first:
                    link(v.tensor_copy(turns, T[11]))
                else:
                    link(v.tensor_tensor(turns, turns, T[11], ALU.add))
                first = False
            round_to(cnt, turns)
            link(v.tensor_tensor(turns, turns, cnt, ALU.subtract))
            pi_a, pi_b = split12(TWO_PI)

            def less_turns(x_):
                round_to(cnt, x_, 1.0 / TWO_PI)
                link(v.scalar_tensor_tensor(x_, cnt, -pi_a, x_, ALU.mult, ALU.add))
                link(v.scalar_tensor_tensor(x_, cnt, -pi_b, x_, ALU.mult, ALU.add))

            less_turns(low)
            link(v.scalar_tensor_tensor(low, turns, TWO_PI, low, ALU.mult, ALU.add))
            LIMIT = 3.1415925
            for n, shift in enumerate((0.0, math.pi / 2)):
                link(v.tensor_scalar(T[n], low, shift, None, ALU.add))
                less_turns(T[n])
            v.tensor_scalar(ropet[:, 0:2, :], ropet[:, 0:2, :], LIMIT, -LIMIT, ALU.min, ALU.max).then_inc(rope_dve, 1)

            lam_sum = [v.tensor_tensor_reduce(out=lam_t[:, n, :], in0=lam_in[:, 2 * n, :], in1=lam_in[:, 2 * n + 1, :],
                                              scale=1.0, scalar=0.0, op0=ALU.mult, op1=ALU.add,
                                              accum_out=lam_e[:, 2 + n:3 + n]) for n in range(2)]
            lam_sum[1].then_inc(lam_exp, 1)

            dve.wait_ge(rope_act, 1)
            for n in range(2):
                for table, src in ((rope_s[n], T[2]), (rope_c[n], T[3])):
                    sv = src.rearrange("p (t i) -> p t i", i=HALF)
                    for hf in range(2):
                        gb = rope_g[:, n:n + 1, hf * HALF:(hf + 1) * HALF].to_broadcast([P, NT, HALF])
                        link(v.tensor_tensor(table[:, :, hf * HALF:(hf + 1) * HALF], sv, gb, ALU.mult))
            def finish_columns():
                dve.wait_ge(rope_act, 2)
                link(v.tensor_tensor(neg_lam[:], lam_e[:, 1:2], lam_e[:, 0:1], ALU.subtract))
                link(v.tensor_scalar(neg_lam[:], neg_lam[:], -LAMBDA_INIT, None, ALU.add))
                dve.wait_ge(gains_loaded, 16 * 9)
                link(v.tensor_scalar(sub_col[:], sub_col[:], 1.0 - LAMBDA_INIT, None, ALU.mult))
                v.tensor_scalar(qk_col[:, 0:1], qk_col[:, 0:1], 1.0 / math.sqrt(QK), None, ALU.mult)\
                    .then_inc(cols_ready, 1)

            def qk_sum(n):
                dve.wait_ge(qk_squared, n + 1)
                if n >= 2:
                    dve.wait_ge(qk_r_done, n - 1)
                link(v.tensor_reduce(qk_ss[:, n % 2, :], qsq[n % 2][:].rearrange("p (g d) -> p g d", d=QK), AX.X, ALU.add))
                v.tensor_scalar(qk_v[:, n % 2, :], qk_ss[:, n % 2, :], 1.0 / QK, EPS, ALU.mult, ALU.add)\
                    .then_inc(qk_v_done, 1)

            def qk_norm(n):
                half, which, t = n // 8, n // 4 % 2, n % 4
                dve.wait_ge(qk_r_done, n + 1)
                full, turn = [P, 4, 2, QK], [P, 4, 2, ROPE]
                r = qk_r[:, n % 2, :].rearrange("p (h m) -> p h m", m=2).unsqueeze(3).to_broadcast(full)
                cos_t = rope_c[which][:, t, :].unsqueeze(1).unsqueeze(1).to_broadcast(turn)
                sin_t = rope_s[which][:, t, :].unsqueeze(1).unsqueeze(1).to_broadcast(turn)
                dst = qkn[:, 4 * half:4 * half + 4, which, t, :].rearrange("p h (m d) -> p h m d", m=2)
                link(v.tensor_tensor(dst, qs[n % 2][:].rearrange("p (h m d) -> p h m d", h=4, m=2), r, ALU.mult))
                rc, rs = (rt[k][:].rearrange("p (h m) d -> p h m d", m=2) for k in range(2))
                link(v.tensor_tensor(rc, dst[:, :, :, 0:ROPE], cos_t, ALU.mult))
                link(v.tensor_tensor(rs, dst[:, :, :, 0:ROPE], sin_t, ALU.mult))
                link(v.tensor_tensor(dst[:, :, :, 0:HALF], rc[:, :, :, 0:HALF], rs[:, :, :, HALF:ROPE], ALU.subtract))
                last = v.tensor_tensor(dst[:, :, :, HALF:ROPE], rc[:, :, :, HALF:ROPE], rs[:, :, :, 0:HALF], ALU.add)
                last.then_inc(qk_ready, 1)

            def v_lo_part(t, n, src):
                dve.wait_ge(v_hi_done, n + 1)
                v.tensor_tensor(v_lo[:, t, :], src[:], f32(v_hi[:, t, :]), ALU.subtract).then_inc(v_lo_done, 1)

            for s in range(AHEAD):
                for t in range(NT):
                    n = NT * s + t
                    if PROJ[s][0] < 2:
                        qk_sum(n)
                        split_lo(s + 1, t, (s + 1) % 2)
                        qk_norm(n)
                    else:
                        split_lo(s + 1, t, (s + 1) % 2)
                        v_lo_part(t, t, bank[n % 4])
                if s == 0:
                    finish_columns()

            def qkT_lo_part(h):
                for n in range(2):
                    dve.wait_ge(qkT_hi_done, 2 * h + n + 1)
                    v.scalar_tensor_tensor(qkT_lo[n][:], bank[n][:], qk_col[:, n:n + 1],
                                           f32(qkT_hi[n][:]), ALU.mult, ALU.subtract).then_inc(qkT_lo_done, 1)

            def maxima(i):
                dve.wait_ge(scored, i + 1)
                if i >= 2:
                    dve.wait_ge(exp_done, 2 * (i - 1))
                for m in range(2):
                    last = v.tensor_reduce(nmax[:, i % 2, m:m + 1], bank[2 * (i % 2) + m][:], AX.X, ALU.max,
                                           negate=True)
                last.then_inc(max_done, 1)

            def combine(i):
                q = i % 2
                dve.wait_ge(exp_done, 2 * i + 2)
                link(v.reciprocal(rl[:, q, :], lsum[:, q, :]))
                v.tensor_copy(rl0[:, i:i + 1], rl[:, q, 0:1])
                link(v.scalar_tensor_tensor(mixc[:, q, :], lsum[:, q, 0:1], neg_lam[:, 0:1], rl[:, q, 1:2],
                                            ALU.mult, ALU.mult))
                v.scalar_tensor_tensor(probs[q][:, 0, :], probs[q][:, 1, :], mixc[:, q, :], probs[q][:, 0, :],
                                       ALU.mult, ALU.add).then_inc(a_done, 1)

            for i in range(LAST):
                if i == TAKE[11]:
                    v_lo_part(3, NT + 3, bank[7])
                if i < STEPS and i % NT:
                    maxima(i)
                if 1 <= i <= STEPS:
                    combine(i - 1)
                if i < STEPS and i % NT == 0:
                    qkT_lo_part(i // NT)
                    maxima(i)
                if i >= 7 and (i - 7) % NT == 0:
                    h = (i - 7) // NT
                    mine = rl0[:, NT * h:NT * h + NT]
                    dve.wait_ge(o_summed, h + 1)
                    link(v.tensor_tensor(o_sq[:], mine, mine, ALU.mult))
                    link(v.tensor_tensor(o_sq[:], bank[5][:, 0:NT], o_sq[:], ALU.mult))
                    v.tensor_scalar(o_v[:], o_sq[:], 1.0 / VD, EPS, ALU.mult, ALU.add).then_inc(o_v_done, 1)
                if i >= 9 and (i - 9) % NT == 0 and (i - 9) // NT < NH:
                    h = (i - 9) // NT
                    dve.wait_ge(o_spread, h + 1)
                    v.tensor_tensor(oc[:], oc[:], bank[5][:], ALU.mult).then_inc(o_normed, 1)
                if i >= 10 and (i - 10) % NT == 0 and (i - 10) // NT < NH:
                    h = (i - 10) // NT
                    dve.wait_ge(oT_hi_done, h + 1)
                    v.scalar_tensor_tensor(oT[h][:, 1, :], oc[:], sub_col[:, 0:1], f32(oT[h][:, 0, :]),
                                           ALU.mult, ALU.subtract).then_inc(oT_lo_done, 1)
                for s, steps in SPLIT.items():
                    for k in range(4):
                        if steps[k] == i:
                            split_lo(s, k, s % 2)
                for f in range(F_V):
                    if TAKE[f] == i:
                        qk_sum(2 * NT + f)
                    if TAKE[f] + 1 == i:
                        qk_norm(2 * NT + f)
                for f in (8, 9, 10):
                    if TAKE[f] == i:
                        v_lo_part(f - 8, NT + f - 8, bank[6 + f % 2])
                for c in range(NC):
                    if FILL[F_X + c, 1] == i:
                        if c == 0:
                            dve.wait_ge(y_added, NC)
                        dve.wait_ge(x_turned, c + 1)
                        v.tensor_tensor(xT[:, c, :], xT[:, c, :], bank[6 + c % 2][:], ALU.add).then_inc(x_added, 1)

            def add_y(t, c, src):
                dve.wait_ge(y_ready, t + 1)
                dve.wait_ge(y_added, t - (NC - 1))
                v.tensor_tensor(xT[:, c, :], xT[:, c, :], src, ALU.add).then_inc(y_added, 1)

            def down_phase(s, slot, y0, width=PIECE, last=False):
                for k in range(4):
                    if not last:
                        split_lo(s + 1, k, 1 - slot, width)
                    for c in (2 * k, 2 * k + 1):
                        add_y(y0 + c, c, bank[4 + c % 4][:])

            dve.wait_ge(x_added, NC)
            down_phase(MLP0 - 1, (MLP0 - 1) % 2, NC)

            def norm_lo(m):
                for c in range(NC):
                    dve.wait_ge(n_hi, NC * m + c + 1)
                    v.scalar_tensor_tensor(hT_lo[:, c, :], xT[:, c, :], gcol[:, m, c:c + 1], f32(hT_hi[:, c, :]),
                                           ALU.mult, ALU.subtract).then_inc(n_lo, 1)

            def norm_v(m):
                dve.wait_ge(n_stat, m + 1)
                v.tensor_scalar(st_v[:, 0:NT], bank[7][:, 0:NT], 1.0 / D, EPS, ALU.mult, ALU.add).then_inc(n_v, 1)

            def norm_diag(m, n):
                dve.wait_ge(n_r, m + 1)
                v.tensor_tensor(z[:, 0, :].rearrange("p (t q) -> p t q", t=NT), ident[:].unsqueeze(1).to_broadcast([P, NT, P]),
                                st_r[:, 0:NT].unsqueeze(2).to_broadcast([P, NT, P]), ALU.mult).then_inc(n_diag, 1)

            def up_phase(s, slot, b, after_split=None):
                if after_split is not None:
                    for f in range(CH):
                        split_lo(s + 1, f, 1 - slot)
                    after_split()
                for f in range(CH):
                    if after_split is None:
                        split_lo(s + 1, f, 1 - slot)
                    dve.wait_ge(h1_ready, b * CH + f + 1)
                    v.scalar_tensor_tensor(z[:, f % 2, :], bank[f][:], 0.0, r_bc[:], ALU.max, ALU.mult)\
                        .then_inc(z_done, 1)
                    dve.wait_ge(zz_done, b * CH + (f + 1))
                    v.tensor_tensor(uT_lo[:, f, :], zz[:, f % 2, :], f32(uT_hi[:, f, :]), ALU.subtract)\
                        .then_inc(u_lo_done, 1)

            for layer in range(2):
                base = MLP_SLAB[layer]
                slot = base % 2
                if layer:
                    norm_lo(1)
                    for k in range(4):
                        split_lo(MLP1, k, MLP1 % 2)
                    norm_v(1)
                    dve.wait_ge(n_r, 2)
                    for gi, w in enumerate(WINDOWS):
                        for t in range(NT):
                            dve.wait_ge(zn_hi_done, NT * gi + (t | 1) + 1)
                            if gi >= 2:
                                dve.wait_ge(pooled, 2 * (gi - 1))
                            v.scalar_tensor_tensor(zn_lo[:, gi % 2, t, :],
                                                   bank[2 * gi + t // 2][:, t % 2 * GW:(t % 2 + 1) * GW],
                                                   st_r[:, t:t + 1], f32(zn_hi[:, gi % 2, t, :]),
                                                   ALU.mult, ALU.subtract).then_inc(zn_lo_done, 1)
                    for c in range(NC):
                        dve.wait_ge(pooled, c + 1)
                        if c >= 2:
                            dve.wait_ge(pool_added, c - 1)
                        if c == 0:
                            dve.wait_ge(band_ready, 1)
                        link(v.scalar_tensor_tensor(zz[:, c % 2, :], bank[c][:], gcol[:, 3, c:c + 1],
                                                    inv_cnt[:, c // 2, :], ALU.mult, ALU.mult))
                        v.tensor_tensor(xT[:, c, :], xT[:, c, :], zz[:, c % 2, :], ALU.add).then_inc(pool_added, 1)
                m = 2 * layer
                norm_lo(m)

                def stats():
                    norm_v(m)
                    norm_diag(m, layer)
                    dve.wait_ge(n_rbc, layer + 1)

                up_phase(base, slot, NB * layer, stats)
                with dve.Fori(0, NB - 1) as j:
                    down_phase(j * 2 + (base + 1), 1 - slot, j * NC + Y_MLP[layer])
                    up_phase(j * 2 + (base + 2), slot, j + (NB * layer + 1))
                down_phase(base + 2 * NB - 1, 1 - slot, Y_MLP[layer] + NC * (NB - 1), 2 * GW, last=layer == 1)

        @block.tensor
        def _(pe):
            def mm(o, lhsT, rhs, start=False, stop=False, **kw):
                return nc.tensor.matmul(o, lhsT, rhs, start=start, stop=stop, **kw)

            def three(o, lh, ll, rh, rl_, start, stop):
                mm(o, lh, rh, start=start)
                mm(o, lh, rl_)
                return mm(o, ll, rh, stop=stop)

            pe.wait_ge(consts, 3)

            def turn_hn(t):
                pe.wait_ge(hn_done, t + 1)
                for half in range(2):
                    n = 2 * t + half
                    if n >= 4:
                        pe.wait_ge(h_lo_done, n - 3)
                    for c in range(4):
                        last = nc.tensor.transpose(bank[4 + n % 4][:, c * P:(c + 1) * P],
                                                   hn[:, t % 2, (4 * half + c) * P:(4 * half + c + 1) * P], ident[:])
                    last.then_inc(hn_turned, 1)

            for t in range(NT):
                turn_hn(t)

            def project(tile, dst, halves=(0, 1)):
                s, t = divmod(tile, NT)
                hi, lo = w_hi[s % 2], w_lo[s % 2]
                for c in range(NC // 2 * halves[0], NC // 2 * (halves[-1] + 1)):
                    if t == 0 and c % 2 == 0:
                        pe.wait_ge(w_lo_done, 4 * s + c // 2 + 1)
                    if s == 0 and c % 4 == 0:
                        pe.wait_ge(h_lo_done, 2 * t + c // 4 + 1)
                    cols = slice(t * P, (t + 1) * P)
                    last = three(dst[:], hT_hi[:, c, cols], hT_lo[:, c, cols],
                                 hi[:, c * BANK:(c + 1) * BANK], lo[:, c * BANK:(c + 1) * BANK],
                                 c == 0, c == NC - 1)
                if halves[-1] == 1:
                    last.then_inc(proj_done, 1)

            for tile in range(NT * AHEAD):
                if tile >= 4:
                    pe.wait_ge(qk_copied, tile - 3)
                project(tile, bank[tile % 4])

            def turn_qk(h):
                for n in range(2):
                    for t in range(NT):
                        last = nc.tensor.transpose(bank[n][:, t * P:(t + 1) * P], qkn[:, h, n, t, :], ident[:])
                    last.then_inc(qk_turned, 1)

            def scores(i):
                t = i % NT
                if t == 0:
                    pe.wait_ge(qkT_lo_done, i // 2 + 2)
                if i >= 2:
                    pe.wait_ge(exp_done, 2 * (i - 1))
                cols = slice(t * P, (t + 1) * P)
                for n, (lhs, rhs) in enumerate(((qkT_hi[0], qkT_hi[1]), (qkT_hi[0], qkT_lo[1]), (qkT_lo[0], qkT_hi[1]))):
                    for m in range(2):
                        rows = slice(m * QK, (m + 1) * QK)
                        last = mm(bank[2 * (i % 2) + m][:], lhs[rows, cols], rhs[rows, :], start=n == 0, stop=n == 2)
                last.then_inc(scored, 1)

            def turn_map(i):
                pe.wait_ge(a_done, i + 1)
                if i:
                    pe.wait_ge(aT_copied, i)
                for k in range(NT):
                    last = nc.tensor.transpose(bank[4][:, k * P:(k + 1) * P], probs[i % 2][:, 0, k * P:(k + 1) * P],
                                               ident[:])
                last.then_inc(a_turned, 1)

            def filler(f, half):
                dst = bank[6 + f % 2]
                if half == 0:
                    g = f - 2
                    if 0 <= g < F_V:
                        pe.wait_ge(qk_copied, 2 * NT + g + 1)
                    elif F_V <= g < F_WO:
                        pe.wait_ge(v_lo_done, NT + g - F_V + 1)
                    elif F_WO <= g < F_X:
                        pe.wait_ge(y_added, g - F_WO + 1)
                    elif g >= F_X:
                        pe.wait_ge(x_added, g - F_X + 1)
                if f < F_WO:
                    project(NT * AHEAD + f, dst, (half,))
                elif f < F_X:
                    c = f - F_WO
                    for k in (2 * half, 2 * half + 1):
                        if c == 0:
                            pe.wait_ge(w_lo_done, 4 * WO0 + k + 1)
                            pe.wait_ge(oT_lo_done, k + 1)
                        cols = slice(k * D + c * P, k * D + (c + 1) * P)
                        last = three(dst[:], w_hi[WO0 % 2][:, cols], w_lo[WO0 % 2][:, cols], oT[k][:, 0, :],
                                     oT[k][:, 1, :], k == 0, k == 3)
                    if half:
                        last.then_inc(y_ready, 1)
                else:
                    c = f - F_X
                    for t in (2 * half, 2 * half + 1):
                        if c == 0:
                            pe.wait_ge(x_again_loaded[t], 16)
                        last = nc.tensor.transpose(dst[:, t * P:(t + 1) * P], x_again[:, t, c * P:(c + 1) * P], ident[:])
                    if half:
                        last.then_inc(x_turned, 1)

            pe.wait_ge(h_lo_done, 2 * NT)
            pe.wait_ge(v_lo_done, NT)
            for i in range(LAST):
                first = i % NT == 0
                if i < STEPS and first:
                    pe.wait_ge(qk_ready, 2 * NT if i < STEPS // 2 else 4 * NT)
                    if i:
                        pe.wait_ge(exp_done, 2 * (i - 1))
                    turn_qk(i // NT)
                if i < STEPS and not first:
                    scores(i)
                if 2 <= i < STEPS + 2:
                    turn_map(i - 2)
                if i >= 6 and (i - 6) % NT == 0 and (i - 6) // NT < NH:
                    h = (i - 6) // NT
                    pe.wait_ge(aT_lo_done, NT * h + NT)
                    if h:
                        pe.wait_ge(o_normed, h)
                    if h == NH // 2:
                        pe.wait_ge(v_lo_done, 2 * NT)
                    cols = slice(h % 4 * VD, (h % 4 + 1) * VD)
                    for k in range(NT):
                        last = three(bank[5][:], v_hi[:, k, cols], v_lo[:, k, cols], aT_hi[:, k, :], aT_lo[:, k, :],
                                     k == 0, k == NT - 1)
                    last.then_inc(pv_done, 1)
                if i >= 7 and (i - 7) % NT == 0 and (i - 7) // NT < NH:
                    h = (i - 7) // NT
                    pe.wait_ge(o_squared, h + 1)
                    for t in range(NT):
                        last = mm(bank[5][:, t:t + 1], osq[:, t * P:(t + 1) * P], ones[:, 0:1], start=True, stop=True)
                    last.then_inc(o_summed, 1)
                if i >= 8 and (i - 8) % NT == 0 and (i - 8) // NT < NH:
                    h = (i - 8) // NT
                    pe.wait_ge(o_diag_done, h + 1)
                    mm(bank[5][:], ones[:], odiag[:].rearrange("p t q -> p (t q)"), start=True, stop=True)\
                        .then_inc(o_spread, 1)
                for (f, half), step in FILL.items():
                    if step == i:
                        filler(f, half)
                if i < STEPS and first:
                    scores(i)

            def down(slot, y0, rhs_hi, rhs_lo, first_w, rhs_wait):
                for pair in range(NC // 2):
                    for ks in ((0, 1, 2), (3,)):
                        for c in (2 * pair, 2 * pair + 1):
                            if ks[0] == 0:
                                if not isinstance(y0, int) or y0 + c >= 4:
                                    pe.wait_ge(y_added, y0 + (c - 3))
                            for k in ks:
                                if pair == 0 and c == 0:
                                    pe.wait_ge(w_lo_done, first_w + (k + 1))
                                    rhs_wait(k)
                                cols = slice(k * D + c * P, k * D + (c + 1) * P)
                                last = three(bank[4 + c % 4][:], w_hi[slot][:, cols], w_lo[slot][:, cols],
                                             rhs_hi(k), rhs_lo(k), k == 0, k == 3)
                            if ks[0] == 3:
                                last.then_inc(y_ready, 1)

            def up(slot, b, first_w, between=None, first=False):
                for f in range(CH):
                    if not first:
                        pe.wait_ge(z_done, b * CH + (f - 3))
                    for c in range(NC):
                        if f == 0 and c % 2 == 0:
                            pe.wait_ge(w_lo_done, first_w + (c // 2 + 1))
                        if f == 0 and between is not None:
                            between(c)
                        cols = slice(c * FB + f * P, c * FB + (f + 1) * P)
                        last = three(bank[f][:], w_hi[slot][:, cols], w_lo[slot][:, cols], hT_hi[:, c, :], hT_lo[:, c, :],
                                     c == 0, c == NC - 1)
                    last.then_inc(h1_ready, 1)
                    yield f

            pe.wait_ge(aT_copied, STEPS)
            pe.wait_ge(o_normed, NH)
            pe.wait_ge(x_added, NC)
            down((MLP0 - 1) % 2, NC, lambda k: oT[4 + k][:, 0, :], lambda k: oT[4 + k][:, 1, :],
                 4 * (MLP0 - 1), lambda k: pe.wait_ge(oT_lo_done, 4 + k + 1))

            def stat(m):
                pe.wait_ge(n_summed, (NC - 1) * (m + 1))
                for t in range(NT):
                    last = mm(bank[7][:, t:t + 1], nsum[:, t * P:(t + 1) * P], ones[:, 0:1], start=True, stop=True)
                last.then_inc(n_stat, 1)

            def spread(n):
                pe.wait_ge(n_diag, n + 1)
                mm(bank[6][:], ones[:], z[:, 0, :], start=True, stop=True).then_inc(n_spread, 1)

            for layer in range(2):
                base = MLP_SLAB[layer]
                slot = base % 2
                m = 2 * layer
                if layer:
                    ps = POOLS % 2

                    def pool_map(gi, ts):
                        for t in ts:
                            for c in range(2):
                                if t == ts[0] and c == 0:
                                    pe.wait_ge(w_lo_done, 4 * POOLS + gi + 1)
                                if t == 0:
                                    pe.wait_ge(n_lo, NC + 2 * gi + c + 1)
                                cols = slice(t * P, (t + 1) * P)
                                wc = slice((2 * gi + c) * GW, (2 * gi + c + 1) * GW)
                                last = three(bank[2 * gi + t // 2][:, t % 2 * GW:(t % 2 + 1) * GW],
                                             hT_hi[:, 2 * gi + c, cols], hT_lo[:, 2 * gi + c, cols],
                                             w_hi[ps][:, wc], w_lo[ps][:, wc], c == 0, c == 1)
                        return last

                    pe.wait_ge(z_done, NB * CH)
                    pe.wait_ge(y_added, Y_MLP[1])
                    for gi in range(3):
                        pool_map(gi, range(NT)).then_inc(zn_ready, 1)
                    stat(1)
                    pool_map(3, range(2))
                    pe.wait_ge(n_v, 2)
                    pool_map(3, range(2, NT)).then_inc(zn_ready, 1)
                    pe.wait_ge(band_ready, 1)
                    for c in range(NC):
                        gi = c // 2
                        pe.wait_ge(zn_lo_done, NT * (gi + 1))
                        for t in range(NT):
                            b0, b1 = max(t * P - PAD, 0), min(t * P + P + PAD, S)
                            c0 = b0 - (t * P - PAD)
                            rhs = band[:, gi, t, c0:c0 + b1 - b0]
                            zc = slice(c % 2 * P, (c % 2 + 1) * P)
                            mm(bank[c][:, b0:b1], zn_hi[:, gi % 2, t, zc], rhs, start=t == 0, skip_group_check=True)
                            last = mm(bank[c][:, b0:b1], zn_lo[:, gi % 2, t, zc], rhs, stop=t == NT - 1,
                                      skip_group_check=True)
                        last.then_inc(pooled, 1)
                    pe.wait_ge(pool_added, NC)

                def need_h(c, m=m):
                    pe.wait_ge(n_lo, NC * m + c + 1)

                for f in up(slot, NB * layer, 4 * base, need_h, first=True):
                    if f == 1:
                        stat(m)
                    if f == 2:
                        spread(layer)
                with pe.Fori(0, NB - 1) as j:
                    down(1 - slot, j * NC + Y_MLP[layer], lambda k: uT_hi[:, k, :], lambda k: uT_lo[:, k, :],
                         j * 8 + 4 * (base + 1),
                         lambda k: pe.wait_ge(u_lo_done, j * CH + (NB * CH * layer + k + 1)))
                    for _ in up(slot, j + (NB * layer + 1), j * 8 + 4 * (base + 2)):
                        pass
                down(1 - slot, NC * (NB - 1) + Y_MLP[layer], lambda k: uT_hi[:, k, :], lambda k: uT_lo[:, k, :],
                     4 * (base + 2 * NB - 1),
                     lambda k: pe.wait_ge(u_lo_done, CH * (NB - 1) + NB * CH * layer + k + 1))
            pe.wait_ge(z_done, 2 * NB * CH)
            for c in range(NC):
                pe.wait_ge(y_added, Y_MLP[1] + NC * (NB - 1) + c + 1)
                if c >= 4:
                    pe.wait_ge(out_kept, c - 3)
                for t in range(NT):
                    last = nc.tensor.transpose(bank[c % 4][:, t * P:(t + 1) * P], xT[:, c, t * P:(t + 1) * P], ident[:])
                last.then_inc(out_turned, 1)


_INS = ["x", "positions", "norm_mix", "norm_mlp", "attn_w_qkv", "attn_w_o", "attn_q_gain", "attn_k_gain",
        "attn_lam_q1", "attn_lam_k1", "attn_lam_q2", "attn_lam_k2", "attn_sub_gain", "pool_w", "pool_scale",
        "mlp_w1", "mlp_w2"]
_ONE_LAYER = {"attn_w_qkv", "attn_w_o", "attn_q_gain", "attn_k_gain", "attn_lam_q1", "attn_lam_k1",
              "attn_lam_q2", "attn_lam_k2", "attn_sub_gain", "pool_w", "pool_scale"}


def kernel(**inputs):
    import concourse.bacc as bacc
    from concourse.bass_utils import run_bass_kernel_spmd

    nc = bacc.Bacc("TRN2", target_bir_lowering=False, num_devices=1, dynamic_dma_scratch_size=1024)
    arrays, args = {}, []
    for name in _INS:
        a = np.ascontiguousarray(inputs[name])
        arrays[f"in_{name}"] = a
        ap = nc.dram_tensor(f"in_{name}", a.shape, mybir.dt.from_np(a.dtype), kind="ExternalInput").ap()
        args.append(ap[0] if name in _ONE_LAYER else ap)
    args.append(nc.dram_tensor("out", (1, S, D), F32, kind="ExternalOutput").ap())
    build_trunk(nc, *args)
    r = run_bass_kernel_spmd(nc, [arrays], core_ids=[0])
    return r.results[0]["out"]
```

```python
import math
from contextlib import ExitStack

import numpy as np

import concourse.bass as bass
from concourse import mybir

F32 = mybir.dt.float32
F32R = mybir.dt.float32r
I32 = mybir.dt.int32
ALU = mybir.AluOpType
ACT = mybir.ActivationFunctionType
AX = mybir.AxisListType

P = 128
D = 1024
S = 512
DFF = 4096
QK = 64
VD = 128
NH = D // VD
ROPE = QK // 4
HALF = ROPE // 2
THETA = 500000.0
WINDOWS = (2, 4, 8, 16)
NG = len(WINDOWS)
GW = D // NG
EPS = 1e-6
NC = D // P
NT = S // P
BANK = 512
SLAB = 8 * BANK
PIECE = SLAB // 4
FB = 512
NB = DFF // FB
CH = FB // P
FIRST = 2
LAMBDA_INIT = 0.8 - 0.6 * math.exp(-0.3 * 0)
PAD = max(WINDOWS) // 2
BW = P + 2 * PAD

STEPS = NH * NT
PROJ = ((0, 0), (1, 0), (2, 0), (0, 1), (1, 1), (2, 1))
AHEAD = 3
F_V, F_Y, F_END = 8, 12, 28


def y_filler(f):
    four, k = divmod(f - F_Y, 4)
    return ("w_o", "x")[k // 2], 2 * four + k % 2


def filler_steps():
    at = {(u // 2, u % 2): u * 11 // 16 for u in range(2 * F_V)}
    at |= {(F_V + u // 2, u % 2): 11 + u * 7 // 8 for u in range(2 * (F_Y - F_V))}
    w_o = ((18, 22), (20, 22), (24, 24), (25, 26), (27, 28), (28, 29), (31, 31), (32, 32))
    turned_x = (23, 23, 26, 27, 30, 30, 33, 33)
    for f in range(F_Y, F_END):
        what, c = y_filler(f)
        at |= {(f, u): w_o[c][u] if what == "w_o" else turned_x[c] for u in range(2)}
    return at


FILL = filler_steps()
TAKE = {f: FILL[f, 1] + 1 for f in range(F_END)}
TAKE |= {f: max(TAKE[f], TAKE[F_V - 1] + 2) for f in range(F_V, F_Y)}
SPLIT = {4: (0, 1, 2, 3), 5: (6, 7, 8, 9), 6: (11, 12, 13, 14), 7: (27, 28, 29, 30), 8: (34, 34, 35, 35)}
LAST = STEPS + 6


def turns():
    seq = [(-1, "q", 0), (-1, "k", 0)]
    for i in range(1, LAST):
        h, phase = divmod(i, NT)
        if 2 <= i < STEPS + 2:
            seq.append((i, "map", i - 2))
        if phase == 1 and h + 1 < NH:
            seq.append((i, "q", h + 1))
        if phase == 2 and h + 1 < NH:
            seq.append((i, "k", h + 1))
        if phase == 0 and 0 <= h - 2 < NH:
            seq.append((i, "o", h - 2))
    return seq


TURNS = turns()
TURN_NO = {(what, n): k for k, (_, what, n) in enumerate(TURNS)}
EXTRA = {step: (what, n) for step, what, n in TURNS if what != "map" and step >= 0}

WO0 = 6
MLP0 = WO0 + 2
POOLS = MLP0 + 2 * NB
MLP1 = POOLS + 1
MLP_SLAB = (MLP0, MLP1)
Y_MLP = (2 * NC, (2 + NB) * NC)


def build_trunk(nc, x, positions, norm_mix, norm_mlp, w_qkv, w_o, q_gain, k_gain, lam_q1, lam_k1,
                lam_q2, lam_k2, sub_gain, pool_w, pool_scale, w1, w2, out):
    ctx = ExitStack()
    with ctx:
        cursor = [-(-nc.sbuf_base // 32) * 32]

        def at(name, shape, dt, offset):
            return nc.alloc_sbuf_tensor_at("s_" + name, shape, dt, offset=offset)

        def size(shape):
            n = 4
            for k in shape[1:]:
                n *= k
            return -(-n // 32) * 32

        def sb(name, shape, dt=F32):
            t = at(name, shape, dt, cursor[0])
            cursor[0] += size(shape)
            return t

        def region(kbytes):
            base = cursor[0]
            cursor[0] += kbytes * 1024
            return base

        def inside(base, *wanted):
            made = []
            for name, shape, dt in wanted:
                made.append(at(name, shape, dt, base))
                base += size(shape)
            return made

        def sem(name):
            return ctx.enter_context(nc.semaphore(name))

        raw = [sb(f"raw{k}", [P, PIECE]) for k in range(4)]
        w_hi = [sb(f"w_hi{k}", [P, SLAB], F32R) for k in range(2)]
        w_lo = [sb(f"w_lo{k}", [P, SLAB], F32R) for k in range(2)]
        x_region = region(16)
        (xT,) = inside(x_region, ("xT", [P, NC, S], F32))
        h_region = region(32)
        qk_region = region(32)
        v_region = region(16)
        scratch = region(34)
        qkT0 = [sb(f"qkT{part}0", [P, 2, S], F32R) for part in ("_hi", "_lo")]

        hT_hi, hT_lo = inside(h_region, ("hT_hi", [P, NC, S], F32R), ("hT_lo", [P, NC, S], F32R))
        x_again, y_part = inside(h_region, ("x_again", [P, NT, D], F32), ("y_part", [P, NC, S], F32))
        (qkn,) = inside(qk_region, ("qkn", [P, NH, 2, NT, P], F32))
        oT = inside(qk_region, *[(f"oT{h}", [P, 2, S], F32R) for h in range(NH)])
        uT_hi, uT_lo, z, zz, r_bc = inside(
            qk_region, ("uT_hi", [P, CH, S], F32R), ("uT_lo", [P, CH, S], F32R),
            ("z", [P, 2, S], F32), ("zz", [P, 2, S], F32), ("r_bc", [P, S], F32))
        zn_hi, zn_lo = inside(qk_region, ("zn_hi", [P, 2, NT, GW], F32R), ("zn_lo", [P, 2, NT, GW], F32R))
        (onat,) = inside(h_region, ("onat", [P, 4, NT, P], F32))
        (val0,) = inside(v_region, ("val0", [P, 2, NT, BANK], F32R))
        (x_nat,) = inside(v_region, ("x_nat", [P, NT, D], F32))
        nsum, nsq, band_lo = inside(v_region, ("nsum", [P, S], F32), ("nsq", [P, 2, S], F32),
                                    ("band_lo", [P, NG, NT, BW], F32R))
        aT_hi, aT_lo, p0, p1, turn_raw, oc, osq, qkT1_hi, qkT1_lo = inside(
            scratch, ("aT_hi", [P, 2, S], F32R), ("aT_lo", [P, 2, S], F32R),
            ("p0", [P, 2, S], F32), ("p1", [P, 2, S], F32), ("turn_raw", [P, 2, S], F32),
            ("oc", [P, 2, S], F32), ("osq", [P, S], F32),
            ("qkT1_hi", [P, 2, S], F32R), ("qkT1_lo", [P, 2, S], F32R))
        qkT_hi, qkT_lo = [qkT0[0], qkT1_hi], [qkT0[1], qkT1_lo]
        probs = [p0, p1]
        hn, g_bc, x_sq, lam_in, lam_t, ropet = inside(
            scratch, ("hn", [P, 2, D], F32), ("g_bc", [P, D], F32), ("x_sq", [P, NT, D], F32),
            ("lam_in", [P, 4, QK], F32), ("lam_t", [P, 2, QK], F32), ("ropet", [P, 16, NT * HALF], F32))
        band_f, band_hi, inv_cnt = inside(
            scratch, ("band_f", [P, NG, NT, BW], F32), ("band_hi", [P, NG, NT, BW], F32R),
            ("inv_cnt", [P, NG, S], F32))
        qs0, qs1, qs2, qs3, qsq0, qsq1, rt0, rt1 = inside(
            x_region, *[(f"qs{k}", [P, S], F32) for k in range(4)], ("qsq0", [P, S], F32), ("qsq1", [P, S], F32),
            ("rt0", [P, 2 * NT, ROPE], F32), ("rt1", [P, 2 * NT, ROPE], F32))
        qs, qsq, rt = [qs0, qs1, qs2, qs3], [qsq0, qsq1], [rt0, rt1]
        (val1,) = inside(x_region, ("val1", [P, 2, NT, BANK], F32R))
        val = [val0, val1]

        ident = sb("ident", [P, P])
        ones = sb("ones", [P, P])
        rope_c = [sb(f"rope_c{n}", [P, NT, ROPE]) for n in "qk"]
        rope_s = [sb(f"rope_s{n}", [P, NT, ROPE]) for n in "qk"]
        minus_half = sb("minus_half", [P, 8])
        gcol = sb("gcol", [P, 4, NC])
        qk_col = sb("qk_col", [P, 2])
        sub_col = sb("sub_col", [P, 1])
        neg_lam = sb("neg_lam", [P, 1])
        lam_e = sb("lam_e", [P, 4])
        in_ss = sb("in_ss", [P, NT])
        in_v = sb("in_v", [P, NT])
        in_r = sb("in_r", [P, NT])
        st_v = sb("st_v", [P, 8])
        st_r = sb("st_r", [P, 8])
        qk_ss = sb("qk_ss", [P, 2, 8])
        qk_v = sb("qk_v", [P, 2, 8])
        qk_r = sb("qk_r", [P, 2, 8])
        nmax = sb("nmax", [P, 2, 2])
        lsum = sb("lsum", [P, 2, 2])
        rl = sb("rl", [P, 2, 2])
        mixc = sb("mixc", [P, 2, 1])
        rl0 = sb("rl0", [P, NH * NT])
        o_ss = sb("o_ss", [P, NT])
        o_sq = sb("o_sq", [P, NT])
        o_v = sb("o_v", [P, NT])
        o_r = sb("o_r", [P, NT])
        o_rl = sb("o_rl", [P, NT])
        posi = sb("posi", [P, NT], I32)
        posf = sb("posf", [P, NT])
        inv_freq = sb("inv_freq", [P, HALF])
        rope_g = sb("rope_g", [P, 2, ROPE])
        assert cursor[0] <= nc.sbuf_usable_end, (cursor[0], nc.sbuf_usable_end)

        bank = [ctx.enter_context(nc.psum_tensor(f"bank{k}", [P, BANK], F32)) for k in range(8)]

        x_loaded = [sem(f"x_loaded{k}") for k in range(NT)]
        small_loaded = sem("small_loaded")
        pos_loaded = sem("pos_loaded")
        rope_loaded = sem("rope_loaded")
        lam_loaded = sem("lam_loaded")
        gains_loaded = sem("gains_loaded")
        raw_loaded = [sem(f"raw_loaded{k}") for k in range(4)]
        stored = [sem(f"stored{k}") for k in range(4)]
        w_hi_done = sem("w_hi_done")
        w_lo_done = sem("w_lo_done")
        consts = sem("consts")
        cols_filled = sem("cols_filled")
        cols_ready = sem("cols_ready")
        sq_done = sem("sq_done")
        v_done = sem("v_done")
        r_done = sem("r_done")
        hn_done = sem("hn_done")
        x_turned = sem("x_turned")
        y_kept = sem("y_kept")
        x_again_loaded = [sem(f"x_again_loaded{k}") for k in range(NT)]
        hn_turned = sem("hn_turned")
        h_hi_done = sem("h_hi_done")
        h_lo_done = sem("h_lo_done")
        proj_done = sem("proj_done")
        qk_copied = sem("qk_copied")
        qk_squared = sem("qk_squared")
        qk_v_done = sem("qk_v_done")
        qk_r_done = sem("qk_r_done")
        qk_ready = sem("qk_ready")
        v_hi_done = sem("v_hi_done")
        v_lo_done = sem("v_lo_done")
        rope_reduced = sem("rope_reduced")
        rope_act = sem("rope_act")
        rope_ready = sem("rope_ready")
        lam_act = sem("lam_act")
        lam_exp = sem("lam_exp")
        scored = sem("scored")
        max_done = sem("max_done")
        exp_done = sem("exp_done")
        a_done = sem("a_done")
        turned = sem("turned")
        turn_kept = sem("turn_kept")
        turn_lo_done = sem("turn_lo_done")
        pv_done = sem("pv_done")
        o_kept = sem("o_kept")
        o_squared = sem("o_squared")
        o_v_done = sem("o_v_done")
        o_normed = sem("o_normed")
        y_ready = sem("y_ready")
        y_added = sem("y_added")
        n_hi = sem("n_hi")
        n_lo = sem("n_lo")
        n_squared = sem("n_squared")
        n_summed = sem("n_summed")
        n_stat = sem("n_stat")
        n_v = sem("n_v")
        n_r = sem("n_r")
        n_diag = sem("n_diag")
        n_spread = sem("n_spread")
        n_rbc = sem("n_rbc")
        h1_ready = sem("h1_ready")
        z_done = sem("z_done")
        zz_done = sem("zz_done")
        u_lo_done = sem("u_lo_done")
        zn_ready = sem("zn_ready")
        zn_hi_done = sem("zn_hi_done")
        zn_lo_done = sem("zn_lo_done")
        band_ready = sem("band_ready")
        pooled = sem("pooled")
        pool_added = sem("pool_added")
        out_turned = sem("out_turned")
        out_kept = sem("out_kept")
        dve_chain = sem("dve_chain")
        pool_chain = sem("pool_chain")

        def wait_used(eng, s):
            if s < 0:
                return
            if s < WO0:
                eng.wait_ge(proj_done, NT * (s + 1))
            elif s < MLP0:
                eng.wait_ge(y_ready, NC * (s - WO0 + 1))
            elif s == POOLS:
                eng.wait_ge(zn_ready, NG)
            else:
                layer = int(s > POOLS)
                j, down = divmod(s - MLP_SLAB[layer], 2)
                if down:
                    eng.wait_ge(y_ready, Y_MLP[layer] + NC * (j + 1))
                else:
                    eng.wait_ge(h1_ready, CH * (NB * layer + j + 1))

        def f32(ap):
            return ap.bitcast(F32)

        def reach(t):
            b0, b1 = max(t * P - PAD, 0), min(t * P + P + PAD, S)
            c0 = b0 - (t * P - PAD)
            return b0, b1, slice(c0, c0 + b1 - b0)

        def turn_dst(what, n):
            if what == "map":
                return aT_hi[:, n % 2, :], aT_lo[:, n % 2, :]
            if what == "o":
                return oT[n][:, 0, :], oT[n][:, 1, :]
            return qkT_hi[n % 2][:, "qk".index(what), :], qkT_lo[n % 2][:, "qk".index(what), :]

        def piece(slab, k):
            if slab < WO0:
                n0 = PROJ[slab][0] * D + PROJ[slab][1] * BANK
                return w_qkv.rearrange("(c p) n -> p c n", p=P)[:, 2 * k:2 * k + 2, n0:n0 + BANK]
            if slab < MLP0:
                return w_o.rearrange("(c p) n -> p c n", p=P)[:, 4 * (slab - WO0) + k, :]
            assert slab == POOLS
            return pool_w[k].rearrange("(c p) n -> p c n", p=P)

        def w1_piece(layer, j, k):
            return w1[layer].rearrange("(c p) n -> p c n", p=P)[:, 2 * k:2 * k + 2, bass.ds(j * FB, FB)]

        def w2_piece(layer, j, k):
            return w2[layer].rearrange("(b k p) n -> p k b n", p=P, k=CH)[:, k, bass.ds(j, 1), :]

        block = ctx.enter_context(nc.Block())

        @block.sync
        def _(sp):
            xv = x.rearrange("a (t p) d -> p (a t) d", p=P)
            for t in range(NT):
                sp.dma_start(x_nat[:, t, :], xv[:, t, :]).then_inc(x_loaded[t], 16)
                sp.dma_start(raw[t][:].rearrange("p (a b) -> p a b", a=2), piece(0, t)).then_inc(raw_loaded[t], 16)

            def load(slab, k, src, width=PIECE):
                sp.wait_ge(w_lo_done, slab * 4 + (k - 3))
                dst = raw[k][:, 0:width]
                if len(src.shape) == 3:
                    dst = dst.rearrange("p (a b) -> p a b", a=src.shape[1])
                sp.dma_start(dst, src).then_inc(raw_loaded[k], 16)

            for s in range(1, MLP0):
                for k in range(4):
                    load(s, k, piece(s, k))
            wait_used(sp, WO0 - 1)
            for t in range(NT):
                sp.dma_start(x_again[:, t, :], xv[:, t, :]).then_inc(x_again_loaded[t], 16)
            for layer in range(2):
                base = MLP_SLAB[layer]
                if layer:
                    for k in range(4):
                        load(POOLS, k, piece(POOLS, k), 2 * GW)
                for k in range(4):
                    load(base, k, w1_piece(layer, 0, k))
                with sp.Fori(0, NB - 1) as j:
                    for k in range(4):
                        load(j * 2 + (base + 1), k, w2_piece(layer, j, k))
                    for k in range(4):
                        load(j * 2 + (base + 2), k, w1_piece(layer, j + 1, k))
                for k in range(4):
                    load(base + 2 * NB - 1, k, w2_piece(layer, NB - 1, k))
            ov = out.rearrange("a (t p) d -> p (a t) d", p=P)
            for c in range(NC):
                sp.wait_ge(out_kept, c + 1)
                sp.dma_start(ov[:, :, c * P:(c + 1) * P], onat[:, c % 4, :, :]).then_inc(stored[c % 4], 16)
            for k in range(4):
                sp.wait_ge(stored[k], 16 * (NC // 4))

        @block.gpsimd
        def _(pool):
            g = nc.gpsimd
            links = [0]

            def link(ins):
                links[0] += 1
                ins.then_inc(pool_chain, 1)
                pool.wait_ge(pool_chain, links[0])

            g.memset(minus_half[:], -0.5).then_inc(consts, 1)
            g.memset(ones[:], 1.0).then_inc(consts, 1)
            link(g.memset(ident[:], 0.0))
            g.affine_select(out=ident[:], in_=ident[:], compare_op=ALU.not_equal, fill=1.0, base=0,
                            pattern=[[-1, P]], channel_multiplier=1).then_inc(consts, 1)
            pool.wait_ge(consts, 1)
            for i in range(HALF):
                freq = g.memset(inv_freq[:, i:i + 1], float(np.float32(THETA ** (-2.0 * i / ROPE))))
            link(freq)

            T = [ropet[:, n, :] for n in range(16)]
            ang, whole, rem, low, turns_, part, cnt = T[4], T[5], T[6], T[7], T[8], T[9], T[10]
            MAGIC = 1.5 * 2.0 ** 23
            TWO_PI = 2.0 * math.pi
            LIMIT = 3.1415925

            def round_to(dst, src, scale=1.0):
                link(g.tensor_scalar(dst, src, scale, MAGIC, ALU.mult, ALU.add))
                link(g.tensor_scalar(dst, dst, -MAGIC, None, ALU.add))

            def split12(c):
                m, e = math.frexp(c)
                a = math.ldexp(round(m * 2 ** 12), e - 12)
                return a, float(np.float32(c - a))

            def axpy(dst, c, a, b, scaled=T[12]):
                link(g.tensor_scalar(scaled, a, c, None, ALU.mult))
                link(g.tensor_tensor(dst, scaled, b, ALU.add))

            def angle_digits():
                pool.wait_ge(pos_loaded, 16)
                link(g.tensor_copy(posf[:], posi[:]))
                link(g.tensor_tensor(ang.rearrange("p (t i) -> p t i", i=HALF),
                                     posf[:].unsqueeze(2).to_broadcast([P, NT, HALF]),
                                     inv_freq[:].unsqueeze(1).to_broadcast([P, NT, HALF]), ALU.mult))
                round_to(whole, ang, 2.0 ** -20)
                axpy(rem, -2.0 ** 20, whole, ang)
                round_to(part, rem, 2.0 ** -8)
                axpy(low, -2.0 ** 8, part, rem)

            def fraction(dst, count, unit):
                frac = unit / TWO_PI
                c_a, c_b = split12(frac - round(frac))
                link(g.tensor_scalar(dst, count, c_a, None, ALU.mult))
                round_to(cnt, dst)
                link(g.tensor_tensor(dst, dst, cnt, ALU.subtract))
                axpy(dst, c_b, count, dst)

            def angle_turns():
                link(g.tensor_tensor(turns_, turns_, T[11], ALU.add))
                round_to(cnt, turns_)
                link(g.tensor_tensor(turns_, turns_, cnt, ALU.subtract))

            def less_turns(x_, count, scaled):
                round_to(count, x_, 1.0 / TWO_PI)
                for part_pi in split12(TWO_PI):
                    axpy(x_, -part_pi, count, x_, scaled)

            def angle_reduced():
                less_turns(low, cnt, T[12])
                axpy(low, TWO_PI, turns_, low)
                for n, shift in enumerate((0.0, math.pi / 2)):
                    link(g.tensor_scalar(T[n], low, shift, None, ALU.add))
                less_turns(ropet[:, 0:2, :], ropet[:, 12:14, :], ropet[:, 14:16, :])
                g.tensor_scalar(ropet[:, 0:2, :], ropet[:, 0:2, :], LIMIT, -LIMIT, ALU.min, ALU.max)\
                    .then_inc(rope_reduced, 1)

            def rope_tables():
                pool.wait_ge(rope_act, 1)
                pool.wait_ge(rope_loaded, 16 * 2)
                for n in range(2):
                    for table, src in ((rope_s[n], T[2]), (rope_c[n], T[3])):
                        sv = src.rearrange("p (t i) -> p t i", i=HALF)
                        for hf in range(2):
                            gb = rope_g[:, n:n + 1, hf * HALF:(hf + 1) * HALF].to_broadcast([P, NT, HALF])
                            link(g.tensor_tensor(table[:, :, hf * HALF:(hf + 1) * HALF], sv, gb, ALU.mult))
                g.memset(st_r[:, 7:8], 0.0).then_inc(rope_ready, 1)

            angle_digits()
            fraction(turns_, whole, 2.0 ** 20)
            fraction(T[11], part, 2.0 ** 8)
            angle_turns()
            angle_reduced()
            pool.wait_ge(v_done, 1)
            g.tensor_tensor(in_r[:], in_v[:], minus_half[:, 0:NT], ALU.pow).then_inc(r_done, 1)
            rope_tables()

            def qk_square(n):
                pool.wait_ge(qk_copied, n + 1)
                if n >= 2:
                    pool.wait_ge(qk_v_done, n - 1)
                g.tensor_tensor(qsq[n % 2][:], qs[n % 4][:], qs[n % 4][:], ALU.mult).then_inc(qk_squared, 1)

            def qk_root(n):
                pool.wait_ge(qk_v_done, n + 1)
                if n >= 2:
                    pool.wait_ge(qk_ready, n - 1)
                g.tensor_tensor(qk_r[:, n % 2, :], qk_v[:, n % 2, :], minus_half[:], ALU.pow)\
                    .then_inc(qk_r_done, 1)

            def turn_lo(what, n):
                k = TURN_NO[what, n]
                hi, lo = turn_dst(what, n)
                pool.wait_ge(turn_kept, k + 1)
                g.tensor_tensor(lo, turn_raw[:, k % 2, :], f32(hi), ALU.subtract).then_inc(turn_lo_done, 1)

            qk_square(0)
            for n in range(1, 2 * NT):
                qk_square(n)
                qk_root(n - 1)
            qk_root(2 * NT - 1)
            turn_lo("q", 0)
            turn_lo("k", 0)
            for i in range(LAST + 1):
                if i - 1 in EXTRA:
                    turn_lo(*EXTRA[i - 1])
                if i >= 7 and (i - 7) % NT == 0:
                    h = (i - 7) // NT
                    pool.wait_ge(o_kept, 2 * h + 2)
                    if h:
                        pool.wait_ge(o_v_done, h)
                    g.tensor_tensor(osq[:], oc[:, h % 2, :], oc[:, h % 2, :], ALU.mult).then_inc(o_squared, 1)
                if i >= 8 and (i - 8) % NT == 0:
                    h = (i - 8) // NT
                    pool.wait_ge(o_v_done, h + 1)
                    link(g.tensor_tensor(o_r[:], o_v[:], minus_half[:, 0:NT], ALU.pow))
                    link(g.tensor_tensor(o_rl[:], o_r[:], rl0[:, NT * h:NT * h + NT], ALU.mult))
                    o_tile = oc[:, h % 2, :].rearrange("p (t d) -> p t d", t=NT)
                    g.tensor_tensor(o_tile, o_tile, o_rl[:].unsqueeze(2).to_broadcast([P, NT, VD]), ALU.mult)\
                        .then_inc(o_normed, 1)
                if 2 <= i < STEPS + 2:
                    turn_lo("map", i - 2)
                for f in range(F_V):
                    if TAKE[f] + 1 == i:
                        qk_root(2 * NT + f)
                for f in range(F_V):
                    if TAKE[f] == i:
                        qk_square(2 * NT + f)

            def norm(m):
                for c in range(NC):
                    pool.wait_ge(n_squared, NC * m + c + 1)
                    if c == 0:
                        if m:
                            pool.wait_ge(n_stat, m)
                        continue
                    first = nsq[:, 0, :] if c == 1 else nsum[:]
                    if c >= 2:
                        pool.wait_ge(n_summed, (NC - 1) * m + c - 1)
                    g.tensor_tensor(nsum[:], first, nsq[:, c % 2, :], ALU.add).then_inc(n_summed, 1)
                pool.wait_ge(n_v, m + 1)
                g.tensor_tensor(st_r[:, 0:NT], st_v[:, 0:NT], minus_half[:, 0:NT], ALU.pow).then_inc(n_r, 1)

            norm(0)
            for gi, w in enumerate(WINDOWS):
                hw = w // 2
                v = band_f[:, gi, :, :]
                link(g.memset(v, 1.0))
                link(g.affine_select(out=v, in_=v, compare_op=ALU.is_ge, fill=0.0, base=PAD + hw,
                                     pattern=[[0, NT], [-1, BW]], channel_multiplier=1))
                link(g.affine_select(out=v, in_=v, compare_op=ALU.is_gt, fill=0.0, base=hw - PAD,
                                     pattern=[[0, NT], [1, BW]], channel_multiplier=-1))
                link(g.affine_select(out=v, in_=v, compare_op=ALU.not_equal, fill=float(1 - w), base=PAD,
                                     pattern=[[0, NT], [-1, BW]], channel_multiplier=1))
                link(g.memset(inv_cnt[:, gi, :], 1.0 / w))
                for t in [*range(hw), *range(S - hw + 1, S)]:
                    cnt = min(t + hw, S) - max(t - hw, 0)
                    tile, col = t // P, t % P + PAD
                    one = band_f[:, gi, tile, col:col + 1]
                    g.affine_select(out=one, in_=one, compare_op=ALU.not_equal, fill=float(1 - cnt),
                                    base=-(t % P), pattern=[[0, 1]], channel_multiplier=1)
                    link(g.memset(inv_cnt[:, gi, t:t + 1], float(np.float32(1.0) / np.float32(cnt))))
                for t in range(NT):
                    b0, b1, cols = reach(t)
                    link(g.tensor_tensor(band_f[:, gi, t, cols], band_f[:, gi, t, cols], inv_cnt[:, gi, b0:b1], ALU.mult))
            for gi in range(NG):
                for t in range(NT):
                    cols = reach(t)[2]
                    link(g.tensor_copy(band_hi[:, gi, t, cols], band_f[:, gi, t, cols]))
                    if t in (0, NT - 1):
                        link(g.tensor_tensor(band_lo[:, gi, t, cols], band_f[:, gi, t, cols],
                                             f32(band_hi[:, gi, t, cols]), ALU.subtract))
            g.memset(st_v[:, 7:8], 0.0).then_inc(band_ready, 1)
            norm(1)
            for k in range(4):
                pool.wait_ge(w_hi_done, 4 * MLP1 + k + 1)
                if k == 0:
                    pool.wait_ge(w_lo_done, 4 * MLP1)
                cols = slice(k * PIECE, (k + 1) * PIECE)
                g.tensor_tensor(w_lo[MLP1 % 2][:, cols], raw[k][:], f32(w_hi[MLP1 % 2][:, cols]), ALU.subtract)\
                    .then_inc(w_lo_done, 1)
            norm(2)

        @block.scalar
        def _(act):
            a = nc.scalar
            act.dma_start(g_bc[:], norm_mix[0].partition_broadcast(P)).then_inc(small_loaded, 16)
            with nc.allow_non_contiguous_dma("positions, 2 KB"):
                act.dma_start(posi[:], positions.rearrange("a (t p) -> p (a t)", p=P)).then_inc(pos_loaded, 16)

            def split_hi(s, k, slot, width=PIECE, free=None):
                act.wait_ge(raw_loaded[k], s * 16 + 16)
                if free is not None:
                    free()
                else:
                    wait_used(act, s - 2)
                a.activation(w_hi[slot][:, k * width:(k + 1) * width], raw[k][:, 0:width], ACT.Copy)\
                    .then_inc(w_hi_done, 1)

            def input_squares(t):
                act.wait_ge(x_loaded[t], 16)
                a.activation(x_sq[:, t, :], x_nat[:, t, :], ACT.Square, accum_out=in_ss[:, t:t + 1])\
                    .then_inc(sq_done, 1)

            def h_hi(n):
                t, half = n // 2, n % 2
                act.wait_ge(hn_turned, n + 1)
                a.activation(hT_hi[:, 4 * half:4 * half + 4, t * P:(t + 1) * P],
                             bank[4 + n % 4][:].rearrange("p (c t) -> p c t", c=4), ACT.Copy)\
                    .then_inc(h_hi_done, 1)

            input_squares(0)
            for t in range(NT):
                split_hi(0, t, 0)
                h_hi(2 * t)
                h_hi(2 * t + 1)
                if t + 1 < NT:
                    input_squares(t + 1)
            with nc.allow_non_contiguous_dma("gains and lambda's vectors, a few KB"):
                for n, gain in enumerate((q_gain, k_gain)):
                    act.dma_start(rope_g[:, n, :], gain[0:ROPE].partition_broadcast(P)).then_inc(rope_loaded, 16)
                for n, lam in enumerate((lam_q1, lam_k1, lam_q2, lam_k2)):
                    act.dma_start(lam_in[:, n, :], lam.partition_broadcast(P)).then_inc(lam_loaded, 16)

            def qk_copy(n, src, tile):
                act.wait_ge(proj_done, tile + 1)
                if n >= 4:
                    act.wait_ge(qk_ready, n - 3)
                if n == 0:
                    act.wait_ge(r_done, 1)
                a.activation(qs[n % 4][:], src[:], ACT.Copy, scale=in_r[:, n % NT:n % NT + 1]).then_inc(qk_copied, 1)

            def v_hi_part(half, t, src, tile):
                act.wait_ge(proj_done, tile + 1)
                if half:
                    act.wait_ge(qk_ready, 4 * NT)
                a.activation(val[half][:, 0, t, :], src[:], ACT.Copy, scale=in_r[:, t:t + 1]).then_inc(v_hi_done, 1)

            def keep_turn(what, n):
                k = TURN_NO[what, n]
                hi, _ = turn_dst(what, n)
                act.wait_ge(turned, k + 1)
                scale = 1.0
                if what == "map":
                    if n >= 2:
                        act.wait_ge(pv_done, n - 1)
                elif what == "o":
                    scale = sub_col[:, 0:1]
                else:
                    if n >= 2:
                        act.wait_ge(scored, NT * (n - 1))
                    scale = qk_col[:, 0:1] if what == "q" else qk_col[:, 1:2]
                a.activation(hi, bank[4][:], ACT.Copy, scale=scale)
                if k >= 2:
                    act.wait_ge(turn_lo_done, k - 1)
                a.activation(turn_raw[:, k % 2, :], bank[4][:], ACT.Copy, scale=scale).then_inc(turn_kept, 1)

            act.wait_ge(rope_reduced, 1)
            a.activation(ropet[:, 2:4, :], ropet[:, 0:2, :], ACT.Sin).then_inc(rope_act, 1)
            for t in range(NT):
                split_hi(1, t, 1)
            for s in range(AHEAD):
                for t in range(NT):
                    if s == 2:
                        split_hi(3, t, 1)
                    tile = NT * s + t
                    if PROJ[s][0] < 2:
                        qk_copy(tile, bank[tile % 4], tile)
                    else:
                        v_hi_part(0, t, bank[tile % 4], tile)
                        if t == 1:
                            act.wait_ge(cols_ready, 1)
                            keep_turn("q", 0)
                        if t == 2:
                            keep_turn("k", 0)
                if s == 0:
                    for t in range(4):
                        split_hi(2, t, 0)
                    act.wait_ge(lam_exp, 1)
                    a.activation(lam_e[:, 0:2], lam_e[:, 2:4], ACT.Exp).then_inc(lam_act, 1)
                    with nc.allow_non_contiguous_dma("gains as columns, a few KB"):
                        act.wait_ge(cols_filled, 1)
                        for n, gain in enumerate((q_gain, k_gain)):
                            for m in range(2):
                                act.dma_start(qk_col[m * QK + ROPE:(m + 1) * QK, n:n + 1],
                                              gain[ROPE:QK].rearrange("(p a) -> p a", a=1)).then_inc(gains_loaded, 16)
                        act.dma_start(sub_col[:], sub_gain.rearrange("(p a) -> p a", a=1)).then_inc(gains_loaded, 16)
                        for n, col in enumerate((norm_mlp[0], norm_mix[1], norm_mlp[1], pool_scale)):
                            act.dma_start(gcol[:, n, :], col.rearrange("(c p) -> p c", p=P)).then_inc(gains_loaded, 16)

            def exps(i):
                act.wait_ge(max_done, i + 1)
                if i >= 2:
                    act.wait_ge(turned, TURN_NO["map", i - 2] + 1)
                for m in range(2):
                    a.activation(probs[i % 2][:, m, :], bank[2 * (i % 2) + m][:], ACT.Exp,
                                 bias=nmax[:, i % 2, m:m + 1],
                                 accum_out=lsum[:, i % 2, m:m + 1]).then_inc(exp_done, 1)

            for i in range(LAST + 1):
                for f in range(F_Y, F_END):
                    what, c = y_filler(f)
                    if TAKE[f] == i and what == "w_o":
                        act.wait_ge(y_ready, c + 1)
                        a.activation(y_part[:, c, :], bank[6 + f % 2][:], ACT.Copy).then_inc(y_kept, 1)
                if 2 <= i < STEPS + 2:
                    keep_turn("map", i - 2)
                if i < STEPS:
                    exps(i)
                if i in EXTRA:
                    keep_turn(*EXTRA[i])
                for f in range(F_Y):
                    if TAKE[f] == i and f < F_V:
                        qk_copy(2 * NT + f, bank[6 + f % 2], NT * AHEAD + f)
                    elif TAKE[f] == i:
                        v_hi_part(1, f - F_V, bank[6 + f % 2], NT * AHEAD + f)
                for s, steps in SPLIT.items():
                    for k in range(4):
                        if steps[k] == i:
                            split_hi(s, k, s % 2)

            def norm_tile(m, c):
                done, count = ((y_added, 2 * NC), (y_added, Y_MLP[1]), (pool_added, NC))[m]
                act.wait_ge(done, count - NC + c + 1)
                a.activation(hT_hi[:, c, :], xT[:, c, :], ACT.Copy, scale=gcol[:, m, c:c + 1]).then_inc(n_hi, 1)
                if m or c >= 2:
                    act.wait_ge(n_summed, (NC - 1) * m + (max(1, c - 2) if c >= 2 else 0))
                a.activation(nsq[:, c % 2, :], xT[:, c, :], ACT.Square).then_inc(n_squared, 1)

            for c in range(NC):
                norm_tile(0, c)

            def spread_copy(m):
                act.wait_ge(n_spread, m + 1)
                a.activation(r_bc[:], bank[6][:], ACT.Copy).then_inc(n_rbc, 1)

            def up_phase(s, slot, b, after_split=None):
                def split(f):
                    split_hi(s + 1, f, 1 - slot, free=lambda: act.wait_ge(y_ready, b * NC + Y_MLP[0]))

                if after_split is not None:
                    for f in range(CH):
                        split(f)
                    after_split()
                for f in range(CH):
                    if after_split is None:
                        split(f)
                    act.wait_ge(z_done, b * CH + (f + 1))
                    a.activation(uT_hi[:, f, :], z[:, f % 2, :], ACT.Square)
                    a.activation(zz[:, f % 2, :], z[:, f % 2, :], ACT.Square).then_inc(zz_done, 1)

            def down_phase(s, slot, b, width=PIECE):
                for k in range(4):
                    split_hi(s + 1, k, 1 - slot, width, free=lambda: act.wait_ge(h1_ready, b * CH + CH))

            for layer in range(2):
                base = MLP_SLAB[layer]
                slot = base % 2
                if layer:
                    for c in range(NC):
                        norm_tile(1, c)

                    def pool_hi(gi):
                        act.wait_ge(zn_ready, gi + 1)
                        if gi >= 2:
                            act.wait_ge(pooled, 2 * (gi - 1))
                        for t in range(NT):
                            a.activation(zn_hi[:, gi % 2, t, :], bank[2 * gi + t // 2][:, t % 2 * GW:(t % 2 + 1) * GW],
                                         ACT.Copy, scale=st_r[:, t:t + 1]).then_inc(zn_hi_done, 1)

                    split_hi(MLP1, 0, MLP1 % 2)
                    split_hi(MLP1, 1, MLP1 % 2)
                    act.wait_ge(n_r, 2)
                    pool_hi(0)
                    pool_hi(1)
                    split_hi(MLP1, 2, MLP1 % 2)
                    pool_hi(2)
                    norm_tile(2, 0)
                    norm_tile(2, 1)
                    pool_hi(3)
                    split_hi(MLP1, 3, MLP1 % 2)
                    for c in range(2, NC):
                        norm_tile(2, c)
                up_phase(base, slot, NB * layer, lambda: spread_copy(layer))
                with act.Fori(0, NB - 1) as j:
                    down_phase(j * 2 + (base + 1), 1 - slot, j + NB * layer)
                    up_phase(j * 2 + (base + 2), slot, j + (NB * layer + 1))
                if layer == 0:
                    down_phase(base + 2 * NB - 1, 1 - slot, NB - 1, 2 * GW)
            for c in range(NC):
                act.wait_ge(out_turned, c + 1)
                if c >= 4:
                    act.wait_ge(stored[c % 4], 16 * (c // 4))
                a.activation(onat[:, c % 4, :, :], bank[c % 4][:].rearrange("p (t c) -> p t c", t=NT), ACT.Copy)\
                    .then_inc(out_kept, 1)

        @block.vector
        def _(dve):
            v = nc.vector
            links = [0]

            def link(ins):
                links[0] += 1
                ins.then_inc(dve_chain, 1)
                dve.wait_ge(dve_chain, links[0])

            v.memset(qk_col[:], 1.0).then_inc(cols_filled, 1)

            def input_gain(t):
                dve.wait_ge(x_loaded[t], 16)
                if t >= 2:
                    dve.wait_ge(hn_turned, 2 * (t - 1))
                v.tensor_tensor(hn[:, t % 2, :], x_nat[:, t, :], g_bc[:], ALU.mult).then_inc(hn_done, 1)

            def h_lo(n):
                t, half = n // 2, n % 2
                dve.wait_ge(h_hi_done, n + 1)
                dst = slice(4 * half, 4 * half + 4), slice(t * P, (t + 1) * P)
                v.tensor_tensor(hT_lo[:, dst[0], dst[1]], bank[4 + n % 4][:].rearrange("p (c t) -> p c t", c=4),
                                f32(hT_hi[:, dst[0], dst[1]]), ALU.subtract).then_inc(h_lo_done, 1)

            def split_lo(s, k, slot, width=PIECE):
                dve.wait_ge(w_hi_done, s * 4 + (k + 1))
                cols = slice(k * width, (k + 1) * width)
                v.tensor_tensor(w_lo[slot][:, cols], raw[k][:, 0:width], f32(w_hi[slot][:, cols]), ALU.subtract)\
                    .then_inc(w_lo_done, 1)

            dve.wait_ge(small_loaded, 16)
            input_gain(0)
            for t in range(NT):
                split_lo(0, t, 0)
                if t + 1 < NT:
                    input_gain(t + 1)
                h_lo(2 * t)
                h_lo(2 * t + 1)

            dve.wait_ge(sq_done, NT)
            v.tensor_scalar(in_v[:], in_ss[:], 1.0 / D, EPS, ALU.mult, ALU.add).then_inc(v_done, 1)
            def finish_columns():
                dve.wait_ge(lam_act, 1)
                link(v.tensor_tensor(neg_lam[:], lam_e[:, 1:2], lam_e[:, 0:1], ALU.subtract))
                link(v.tensor_scalar(neg_lam[:], neg_lam[:], -LAMBDA_INIT, None, ALU.add))
                dve.wait_ge(gains_loaded, 16 * 9)
                link(v.tensor_scalar(sub_col[:], sub_col[:], 1.0 - LAMBDA_INIT, None, ALU.mult))
                v.tensor_scalar(qk_col[:, 0:1], qk_col[:, 0:1], 1.0 / math.sqrt(QK), None, ALU.mult)\
                    .then_inc(cols_ready, 1)

            def qk_sum(n):
                dve.wait_ge(qk_squared, n + 1)
                if n >= 2:
                    dve.wait_ge(qk_r_done, n - 1)
                link(v.tensor_reduce(qk_ss[:, n % 2, :], qsq[n % 2][:].rearrange("p (g d) -> p g d", d=QK), AX.X, ALU.add))
                v.tensor_scalar(qk_v[:, n % 2, :], qk_ss[:, n % 2, :], 1.0 / QK, EPS, ALU.mult, ALU.add)\
                    .then_inc(qk_v_done, 1)

            def qk_norm(n):
                half, which, t = n // 8, n // 4 % 2, n % 4
                dve.wait_ge(qk_r_done, n + 1)
                full, turn = [P, 4, 2, QK], [P, 4, 2, ROPE]
                r = qk_r[:, n % 2, :].rearrange("p (h m) -> p h m", m=2).unsqueeze(3).to_broadcast(full)
                cos_t = rope_c[which][:, t, :].unsqueeze(1).unsqueeze(1).to_broadcast(turn)
                sin_t = rope_s[which][:, t, :].unsqueeze(1).unsqueeze(1).to_broadcast(turn)
                dst = qkn[:, 4 * half:4 * half + 4, which, t, :].rearrange("p h (m d) -> p h m d", m=2)
                link(v.tensor_tensor(dst, qs[n % 4][:].rearrange("p (h m d) -> p h m d", h=4, m=2), r, ALU.mult))
                rc, rs = (rt[k][:].rearrange("p (h m) d -> p h m d", m=2) for k in range(2))
                if n == 0:
                    dve.wait_ge(rope_ready, 1)
                link(v.tensor_tensor(rc, dst[:, :, :, 0:ROPE], cos_t, ALU.mult))
                link(v.tensor_tensor(rs, dst[:, :, :, 0:ROPE], sin_t, ALU.mult))
                link(v.tensor_tensor(dst[:, :, :, 0:HALF], rc[:, :, :, 0:HALF], rs[:, :, :, HALF:ROPE], ALU.subtract))
                last = v.tensor_tensor(dst[:, :, :, HALF:ROPE], rc[:, :, :, HALF:ROPE], rs[:, :, :, 0:HALF], ALU.add)
                last.then_inc(qk_ready, 1)

            def v_lo_part(half, t, src):
                dve.wait_ge(v_hi_done, NT * half + t + 1)
                v.scalar_tensor_tensor(val[half][:, 1, t, :], src[:], in_r[:, t:t + 1], f32(val[half][:, 0, t, :]),
                                       ALU.mult, ALU.subtract)\
                    .then_inc(v_lo_done, 1)

            for t in range(NT):
                split_lo(1, t, 1)
            for s in range(AHEAD):
                for t in range(NT):
                    n = NT * s + t
                    if s == 2:
                        split_lo(3, t, 1)
                    if n < 2 * NT:
                        qk_sum(n)
                    if 1 <= n <= 2 * NT:
                        qk_norm(n - 1)
                    if s == 0:
                        split_lo(2, t, 0)
                    if n >= 2 * NT:
                        v_lo_part(0, t, bank[n % 4])
                if s == 0:
                    dve.wait_ge(lam_loaded, 16 * 4)
                    lam_sum = [v.tensor_tensor_reduce(out=lam_t[:, n, :], in0=lam_in[:, 2 * n, :],
                                                      in1=lam_in[:, 2 * n + 1, :], scale=1.0, scalar=0.0,
                                                      op0=ALU.mult, op1=ALU.add,
                                                      accum_out=lam_e[:, 2 + n:3 + n]) for n in range(2)]
                    lam_sum[1].then_inc(lam_exp, 1)
                if s == 1:
                    finish_columns()

            def maxima(i):
                dve.wait_ge(scored, i + 1)
                if i >= 2:
                    dve.wait_ge(exp_done, 2 * (i - 1))
                for m in range(2):
                    last = v.tensor_reduce(nmax[:, i % 2, m:m + 1], bank[2 * (i % 2) + m][:], AX.X, ALU.max,
                                           negate=True)
                last.then_inc(max_done, 1)

            def o_keep(n):
                h, pair = divmod(n, 2)
                dve.wait_ge(pv_done, 2 * n + 2)
                if h >= 2 and pair == 0:
                    dve.wait_ge(turned, TURN_NO["o", h - 2] + 1)
                v.tensor_reduce(oc[:, h % 2, 2 * pair * VD:(2 * pair + 2) * VD].rearrange("p (t d) -> p t d", t=2),
                                bank[5][:].rearrange("p (t m d) -> p t d m", t=2, m=2), AX.X, ALU.add)\
                    .then_inc(o_kept, 1)

            def combine(i):
                q = i % 2
                dve.wait_ge(exp_done, 2 * i + 2)
                link(v.reciprocal(rl[:, q, :], lsum[:, q, :]))
                v.tensor_copy(rl0[:, i:i + 1], rl[:, q, 0:1])
                link(v.scalar_tensor_tensor(mixc[:, q, :], lsum[:, q, 0:1], neg_lam[:, 0:1], rl[:, q, 1:2],
                                            ALU.mult, ALU.mult))
                v.scalar_tensor_tensor(probs[q][:, 0, :], probs[q][:, 1, :], mixc[:, q, :], probs[q][:, 0, :],
                                       ALU.mult, ALU.add).then_inc(a_done, 1)

            for i in range(LAST + 1):
                for f in range(F_V, F_Y):
                    if TAKE[f] + 1 == i:
                        v_lo_part(1, f - F_V, bank[6 + f % 2])
                for f in range(F_Y, F_END):
                    what, c = y_filler(f)
                    if TAKE[f] == i and what == "x":
                        dve.wait_ge(y_kept, c + 1)
                        dve.wait_ge(x_turned, c + 1)
                        v.tensor_tensor(y_part[:, c, :], y_part[:, c, :], bank[6 + f % 2][:], ALU.add)\
                            .then_inc(y_added, 1)
                if i >= 5 and i % 2 and (i - 5) // 2 < 2 * NH:
                    o_keep((i - 5) // 2)
                if i < STEPS:
                    maxima(i)
                if 1 <= i <= STEPS:
                    combine(i - 1)
                if i >= 7 and (i - 7) % NT == 0:
                    h = (i - 7) // NT
                    mine = rl0[:, NT * h:NT * h + NT]
                    link(v.tensor_tensor(o_sq[:], mine, mine, ALU.mult))
                    dve.wait_ge(o_squared, h + 1)
                    link(v.tensor_reduce(o_ss[:], osq[:].rearrange("p (t d) -> p t d", t=NT), AX.X, ALU.add))
                    link(v.tensor_tensor(o_sq[:], o_ss[:], o_sq[:], ALU.mult))
                    if h:
                        dve.wait_ge(o_normed, h)
                    v.tensor_scalar(o_v[:], o_sq[:], 1.0 / VD, EPS, ALU.mult, ALU.add).then_inc(o_v_done, 1)
                for f in range(F_V):
                    if TAKE[f] + 1 == i:
                        qk_sum(2 * NT + f)
                    if TAKE[f] + 2 == i:
                        qk_norm(2 * NT + f)
                for s, steps in SPLIT.items():
                    for k in range(4):
                        if steps[k] + 1 == i:
                            split_lo(s, k, s % 2)

            def add_y(t, c, src, old=None):
                old = xT if old is None else old
                dve.wait_ge(y_ready, t + 1)
                dve.wait_ge(y_added, t - (NC - 1))
                v.tensor_tensor(xT[:, c, :], old[:, c, :], src, ALU.add).then_inc(y_added, 1)

            def down_phase(s, slot, y0, width=PIECE, then="up"):
                for k in range(4):
                    if then != "end":
                        split_lo(s + 1, k, 1 - slot, width)
                    for c in (2 * k, 2 * k + 1):
                        add_y(y0 + c, c, bank[4 + c % 4][:])
                        if then == "pooling" and c:
                            norm_lo(1, c - 1)
                if then == "pooling":
                    norm_lo(1, NC - 1)

            def norm_lo(m, c):
                dve.wait_ge(n_hi, NC * m + c + 1)
                v.scalar_tensor_tensor(hT_lo[:, c, :], xT[:, c, :], gcol[:, m, c:c + 1], f32(hT_hi[:, c, :]),
                                       ALU.mult, ALU.subtract).then_inc(n_lo, 1)

            dve.wait_ge(pv_done, STEPS)
            for c in range(NC):
                add_y(NC + c, c, bank[c][:], y_part)
                if c:
                    norm_lo(0, c - 1)
            norm_lo(0, NC - 1)

            def norm_v(m):
                dve.wait_ge(n_stat, m + 1)
                v.tensor_scalar(st_v[:, 0:NT], bank[7][:, 0:NT], 1.0 / D, EPS, ALU.mult, ALU.add).then_inc(n_v, 1)

            def norm_diag(m, n):
                dve.wait_ge(n_r, m + 1)
                v.tensor_tensor(z[:, 0, :].rearrange("p (t q) -> p t q", t=NT),
                                ident[:].unsqueeze(1).to_broadcast([P, NT, P]),
                                st_r[:, 0:NT].unsqueeze(2).to_broadcast([P, NT, P]), ALU.mult).then_inc(n_diag, 1)

            def up_phase(s, slot, b, first=None):

                def hidden(f):
                    dve.wait_ge(h1_ready, b * CH + f + 1)
                    if first is not None and f >= 2:
                        dve.wait_ge(zz_done, b * CH + (f - 1))
                    v.scalar_tensor_tensor(z[:, f % 2, :], bank[f][:], 0.0, r_bc[:], ALU.max, ALU.mult)\
                        .then_inc(z_done, 1)

                def hidden_lo(f):
                    dve.wait_ge(zz_done, b * CH + (f + 1))
                    v.tensor_tensor(uT_lo[:, f, :], zz[:, f % 2, :], f32(uT_hi[:, f, :]), ALU.subtract)\
                        .then_inc(u_lo_done, 1)

                if first is None:
                    for f in range(CH):
                        split_lo(s + 1, f, 1 - slot)
                        hidden(f)
                        hidden_lo(f)
                else:
                    norm_v(first)
                    dve.wait_ge(w_lo_done, 4 * (s + 1))
                    split_lo(s + 1, 0, 1 - slot)
                    norm_diag(first, first // 2)
                    split_lo(s + 1, 1, 1 - slot)
                    dve.wait_ge(n_rbc, first // 2 + 1)
                    hidden(0)
                    split_lo(s + 1, 2, 1 - slot)
                    hidden(1)
                    hidden_lo(0)
                    split_lo(s + 1, 3, 1 - slot)
                    for f in range(2, CH):
                        hidden(f)
                        hidden_lo(f - 1)
                    hidden_lo(CH - 1)

            for layer in range(2):
                base = MLP_SLAB[layer]
                slot = base % 2
                if layer:
                    def pool_lo(gi):
                        for t in range(NT):
                            dve.wait_ge(zn_hi_done, NT * gi + (t | 1) + 1)
                            if gi >= 2:
                                dve.wait_ge(pooled, 2 * (gi - 1))
                            v.scalar_tensor_tensor(zn_lo[:, gi % 2, t, :],
                                                   bank[2 * gi + t // 2][:, t % 2 * GW:(t % 2 + 1) * GW],
                                                   st_r[:, t:t + 1], f32(zn_hi[:, gi % 2, t, :]),
                                                   ALU.mult, ALU.subtract).then_inc(zn_lo_done, 1)

                    def pool_add(c):
                        dve.wait_ge(pooled, c + 1)
                        v.scalar_tensor_tensor(xT[:, c, :], bank[c][:], gcol[:, 3, c:c + 1], xT[:, c, :],
                                               ALU.mult, ALU.add).then_inc(pool_added, 1)
                        if c:
                            norm_lo(2, c - 1)

                    norm_v(1)
                    dve.wait_ge(n_r, 2)
                    pool_lo(0)
                    pool_lo(1)
                    pool_add(0)
                    pool_add(1)
                    pool_lo(2)
                    pool_add(2)
                    pool_lo(3)
                    for c in range(3, NC):
                        pool_add(c)
                    norm_lo(2, NC - 1)
                up_phase(base, slot, NB * layer, first=2 * layer)
                with dve.Fori(0, NB - 1) as j:
                    down_phase(j * 2 + (base + 1), 1 - slot, j * NC + Y_MLP[layer])
                    up_phase(j * 2 + (base + 2), slot, j + (NB * layer + 1))
                down_phase(base + 2 * NB - 1, 1 - slot, Y_MLP[layer] + NC * (NB - 1), 2 * GW,
                           "end" if layer else "pooling")

        @block.tensor
        def _(pe):
            def mm(o, lhsT, rhs, start=False, stop=False, **kw):
                return nc.tensor.matmul(o, lhsT, rhs, start=start, stop=stop, **kw)

            def three(o, lh, ll, rh, rl_, start, stop):
                mm(o, lh, rh, start=start)
                mm(o, lh, rl_)
                return mm(o, ll, rh, stop=stop)

            pe.wait_ge(consts, 3)

            def turn_hn(t):
                pe.wait_ge(hn_done, t + 1)
                for half in range(2):
                    n = 2 * t + half
                    if n >= 4:
                        pe.wait_ge(h_lo_done, n - 3)
                    for c in range(4):
                        last = nc.tensor.transpose(bank[4 + n % 4][:, c * P:(c + 1) * P],
                                                   hn[:, t % 2, (4 * half + c) * P:(4 * half + c + 1) * P], ident[:])
                    last.then_inc(hn_turned, 1)

            def project(tile, dst, pieces=range(4)):
                s, t = divmod(tile, NT)
                hi, lo = w_hi[s % 2], w_lo[s % 2]
                for c in range(2 * pieces[0], 2 * pieces[-1] + 2):
                    if t == 0 and c % 2 == 0:
                        pe.wait_ge(w_lo_done, 4 * s + c // 2 + 1)
                    if s == 0 and c % 4 == 0:
                        pe.wait_ge(h_lo_done, 2 * t + c // 4 + 1)
                    cols = slice(t * P, (t + 1) * P)
                    last = three(dst[:], hT_hi[:, c, cols], hT_lo[:, c, cols],
                                 hi[:, c * BANK:(c + 1) * BANK], lo[:, c * BANK:(c + 1) * BANK],
                                 c == 0, c == NC - 1)
                if pieces[-1] == 3:
                    last.then_inc(proj_done, 1)

            def turn(what, n):
                k = TURN_NO[what, n]
                if what == "map":
                    pe.wait_ge(a_done, n + 1)
                    src = [probs[n % 2][:, 0, t * P:(t + 1) * P] for t in range(NT)]
                elif what == "o":
                    pe.wait_ge(o_normed, n + 1)
                    src = [oc[:, n % 2, t * P:(t + 1) * P] for t in range(NT)]
                else:
                    which = "qk".index(what)
                    pe.wait_ge(qk_ready, 2 * NT * (n // (NH // 2)) + NT * which + NT)
                    src = [qkn[:, n, which, t, :] for t in range(NT)]
                if k:
                    pe.wait_ge(turn_kept, k)
                else:
                    pe.wait_ge(h_lo_done, 2 * NT)
                for t in range(NT):
                    last = nc.tensor.transpose(bank[4][:, t * P:(t + 1) * P], src[t], ident[:])
                last.then_inc(turned, 1)

            turn_hn(0)
            for t, pieces in ((0, (0,)), (0, (1,)), (1, (0, 1)), (0, (2,)), (1, (2,)), (2, (0, 1, 2)),
                              (0, (3,)), (1, (3,)), (2, (3,)), (3, (0, 1, 2, 3))):
                project(t, bank[t], pieces)
                if (t, pieces[-1]) in ((0, 0), (1, 1), (2, 2)):
                    turn_hn(t + 1)
            for tile in range(NT, NT * AHEAD):
                if tile >= 4:
                    pe.wait_ge(qk_copied, tile - 3)
                project(tile, bank[tile % 4])
                if tile == 2 * NT + 1:
                    turn("q", 0)
                if tile == 2 * NT + 2:
                    turn("k", 0)

            def scores(i):
                h, t = divmod(i, NT)
                hi, lo = qkT_hi[h % 2], qkT_lo[h % 2]
                if t == 0:
                    pe.wait_ge(turn_lo_done, TURN_NO["k", h] + 1)
                if i >= 2:
                    pe.wait_ge(exp_done, 2 * (i - 1))
                cols = slice(t * P, (t + 1) * P)
                for n, (lhs, rhs) in enumerate(((hi, hi), (hi, lo), (lo, hi))):
                    for m in range(2):
                        rows = slice(m * QK, (m + 1) * QK)
                        last = mm(bank[2 * (i % 2) + m][:], lhs[rows, 0, cols], rhs[rows, 1, :], start=n == 0, stop=n == 2)
                last.then_inc(scored, 1)

            def values(i):
                h, t = divmod(i, NT)
                half = h // (NH // 2)
                pe.wait_ge(turn_lo_done, TURN_NO["map", i] + 1)
                if t == 0:
                    pe.wait_ge(v_lo_done, NT * (half + 1))
                if t % 2 == 0 and i:
                    pe.wait_ge(o_kept, i // 2)
                cols = slice(h % 4 * VD, (h % 4 + 1) * VD)
                main = t % 2 * 2 * VD
                for k in range(NT):
                    keys = slice(k * P, (k + 1) * P)
                    mm(bank[5][:, main:main + 2 * VD], aT_hi[:, i % 2, keys], val[half][:, :, k, cols],
                       start=k == 0, skip_group_check=True)
                    last = mm(bank[5][:, main:main + VD], aT_lo[:, i % 2, keys], val[half][:, 0, k, cols],
                              stop=k == NT - 1, skip_group_check=True)
                last.then_inc(pv_done, 1)

            def filler(f, half):
                dst = bank[6 + f % 2]
                if half == 0:
                    g = f - 2
                    if 0 <= g < F_V:
                        pe.wait_ge(qk_copied, 2 * NT + g + 1)
                    elif F_V <= g < F_Y:
                        pe.wait_ge(v_lo_done, NT + g - F_V + 1)
                    elif g >= F_Y:
                        what, c = y_filler(g)
                        pe.wait_ge(y_kept if what == "w_o" else y_added, c + 1)
                what, c = ("projection", 0) if f < F_Y else y_filler(f)
                if f < F_Y:
                    project(NT * AHEAD + f, dst, (2 * half, 2 * half + 1))
                elif what == "w_o":
                    for k in (2 * half, 2 * half + 1):
                        if c == 0:
                            pe.wait_ge(w_lo_done, 4 * WO0 + k + 1)
                            pe.wait_ge(turn_lo_done, TURN_NO["o", k] + 1)
                        cols = slice(k * D + c * P, k * D + (c + 1) * P)
                        last = three(dst[:], w_hi[WO0 % 2][:, cols], w_lo[WO0 % 2][:, cols], oT[k][:, 0, :],
                                     oT[k][:, 1, :], k == 0, k == 3)
                    if half:
                        last.then_inc(y_ready, 1)
                else:
                    for t in (2 * half, 2 * half + 1):
                        if c == 0:
                            pe.wait_ge(x_again_loaded[t], 16)
                        last = nc.tensor.transpose(dst[:, t * P:(t + 1) * P], x_again[:, t, c * P:(c + 1) * P], ident[:])
                    if half:
                        last.then_inc(x_turned, 1)

            def w_o_rest(cs, ks):
                s = WO0 + 1
                for c in cs:
                    for k in ks:
                        if c == 0:
                            pe.wait_ge(w_lo_done, 4 * s + k + 1)
                            pe.wait_ge(turn_lo_done, TURN_NO["o", 4 + k] + 1)
                        cols = slice(k * D + c * P, k * D + (c + 1) * P)
                        last = three(bank[c][:], w_hi[s % 2][:, cols], w_lo[s % 2][:, cols], oT[4 + k][:, 0, :],
                                     oT[4 + k][:, 1, :], k == 0, k == 3)
                    if ks[-1] == 3:
                        last.then_inc(y_ready, 1)

            for i in range(LAST):
                if i < 2:
                    pe.wait_ge(v_lo_done, 2 * i + 2)
                now = [part for part, step in FILL.items() if step == i]
                if i < STEPS:
                    scores(i)
                if i == STEPS + 1:
                    pe.wait_ge(exp_done, 2 * (STEPS - 1))
                    w_o_rest((0, 1), (0, 1))
                if i == STEPS + 2:
                    pe.wait_ge(exp_done, 2 * STEPS)
                    w_o_rest((2, 3), (0, 1))
                if 2 <= i < STEPS + 2:
                    turn("map", i - 2)
                for part in now[:1]:
                    filler(*part)
                if i in EXTRA and i < STEPS:
                    turn(*EXTRA[i])
                if 3 <= i < STEPS + 3:
                    values(i - 3)
                for part in now[1:]:
                    filler(*part)
                if i == STEPS + 3:
                    w_o_rest(range(4), (2,))
                    pe.wait_ge(y_added, NC)
                    w_o_rest((6, 7), (0, 1, 2))
                if i in EXTRA and i >= STEPS:
                    turn(*EXTRA[i])

            def down(slot, y0, rhs_hi, rhs_lo, first_w, rhs_wait, last_pairs=None):
                for pair in range(NC // 2):
                    for ks in ((0, 1, 2), (3,)):
                        if ks[0] == 3 and last_pairs is not None:
                            last_pairs(pair)
                        for c in (2 * pair, 2 * pair + 1):
                            if ks[0] == 0:
                                if not isinstance(y0, int) or y0 + c >= 4:
                                    pe.wait_ge(y_added, y0 + (c - 3))
                            for k in ks:
                                if pair == 0 and c == 0:
                                    pe.wait_ge(w_lo_done, first_w + (k + 1))
                                    rhs_wait(k)
                                cols = slice(k * D + c * P, k * D + (c + 1) * P)
                                last = three(bank[4 + c % 4][:], w_hi[slot][:, cols], w_lo[slot][:, cols],
                                             rhs_hi(k), rhs_lo(k), k == 0, k == 3)
                            if ks[0] == 3:
                                last.then_inc(y_ready, 1)

            def up_part(slot, f, c):
                cols = slice(c * FB + f * P, c * FB + (f + 1) * P)
                last = three(bank[f][:], w_hi[slot][:, cols], w_lo[slot][:, cols], hT_hi[:, c, :], hT_lo[:, c, :],
                             c == 0, c == NC - 1)
                if c == NC - 1:
                    last.then_inc(h1_ready, 1)

            def up(slot, b, first_w):
                for f in range(CH):
                    pe.wait_ge(z_done, b * CH + (f - 3))
                    for c in range(NC):
                        if f == 0 and c % 2 == 0:
                            pe.wait_ge(w_lo_done, first_w + (c // 2 + 1))
                        up_part(slot, f, c)

            def first_tiles(layer, slot, first_w, cs):
                m = 2 * layer
                for c in cs:
                    pe.wait_ge(n_lo, NC * m + c + 1)
                    if c % 2 == 0:
                        pe.wait_ge(w_lo_done, first_w + c // 2 + 1)
                    for f in range(min(c + 1, FIRST)):
                        for c2 in range(c + 1) if f == c else (c,):
                            up_part(slot, f, c2)

            def first_rest(layer, slot):
                stat(2 * layer)
                rest = [(f, c) for f in range(FIRST, CH) for c in range(NC)]
                for n, (f, c) in enumerate(rest):
                    if n == NC // 2:
                        spread(layer)
                    up_part(slot, f, c)

            pe.wait_ge(o_kept, 2 * NH)
            w_o_rest((5,), (0, 1, 2))
            w_o_rest(range(4), (3,))
            pe.wait_ge(turn_kept, len(TURNS))
            w_o_rest((4,), (0, 1, 2, 3))
            w_o_rest((5, 6, 7), (3,))

            def stat(m):
                pe.wait_ge(n_summed, (NC - 1) * (m + 1))
                for t in range(NT):
                    last = mm(bank[7][:, t:t + 1], nsum[:, t * P:(t + 1) * P], ones[:, 0:1], start=True, stop=True)
                last.then_inc(n_stat, 1)

            def spread(n):
                pe.wait_ge(n_diag, n + 1)
                mm(bank[6][:], ones[:], z[:, 0, :], start=True, stop=True).then_inc(n_spread, 1)

            def turn_out(pair):
                if pair == 0:
                    pe.wait_ge(z_done, 2 * NB * CH)
                    return
                for c in (2 * pair - 2, 2 * pair - 1):
                    pe.wait_ge(y_added, Y_MLP[1] + NC * (NB - 1) + c + 1)
                    if c >= 4:
                        pe.wait_ge(out_kept, c - 3)
                    for t in range(NT):
                        last = nc.tensor.transpose(bank[c % 4][:, t * P:(t + 1) * P], xT[:, c, t * P:(t + 1) * P], ident[:])
                    last.then_inc(out_turned, 1)

            for layer in range(2):
                base = MLP_SLAB[layer]
                slot = base % 2
                if layer:
                    ps = POOLS % 2

                    def pool_map(gi, ts):
                        for t in ts:
                            for c in range(2):
                                if t == ts[0] and c == 0:
                                    pe.wait_ge(w_lo_done, 4 * POOLS + gi + 1)
                                if t == 0:
                                    pe.wait_ge(n_lo, NC + 2 * gi + c + 1)
                                cols = slice(t * P, (t + 1) * P)
                                wc = slice((2 * gi + c) * GW, (2 * gi + c + 1) * GW)
                                last = three(bank[2 * gi + t // 2][:, t % 2 * GW:(t % 2 + 1) * GW],
                                             hT_hi[:, 2 * gi + c, cols], hT_lo[:, 2 * gi + c, cols],
                                             w_hi[ps][:, wc], w_lo[ps][:, wc], c == 0, c == 1)
                        return last

                    def windows(c):
                        gi = c // 2
                        for t in range(NT):
                            b0, b1, cols = reach(t)
                            zc = slice(c % 2 * P, (c % 2 + 1) * P)
                            mm(bank[c][:, b0:b1], zn_hi[:, gi % 2, t, zc], band_hi[:, gi, t, cols], start=t == 0,
                               skip_group_check=True)
                            if t in (0, NT - 1):
                                mm(bank[c][:, b0:b1], zn_hi[:, gi % 2, t, zc], band_lo[:, gi, t, cols],
                                   skip_group_check=True)
                            last = mm(bank[c][:, b0:b1], zn_lo[:, gi % 2, t, zc], band_hi[:, gi, t, cols],
                                      stop=t == NT - 1, skip_group_check=True)
                        last.then_inc(pooled, 1)

                    pe.wait_ge(z_done, NB * CH)
                    pool_map(0, range(NT)).then_inc(zn_ready, 1)
                    pool_map(1, range(NT)).then_inc(zn_ready, 1)
                    pe.wait_ge(y_added, Y_MLP[1])
                    stat(1)
                    pool_map(2, range(NT)).then_inc(zn_ready, 1)
                    pe.wait_ge(band_ready, 1)
                    for gi in range(NG):
                        if gi == 3:
                            first_tiles(layer, slot, 4 * base, range(2))
                        pe.wait_ge(zn_lo_done, NT * (gi + 1))
                        windows(2 * gi)
                        windows(2 * gi + 1)
                        if gi == 0:
                            pe.wait_ge(n_v, 2)
                            pool_map(3, range(NT)).then_inc(zn_ready, 1)

                first_tiles(layer, slot, 4 * base, range(2 * layer, NC))
                first_rest(layer, slot)
                with pe.Fori(0, NB - 1) as j:
                    down(1 - slot, j * NC + Y_MLP[layer], lambda k: uT_hi[:, k, :], lambda k: uT_lo[:, k, :],
                         j * 8 + 4 * (base + 1),
                         lambda k: pe.wait_ge(u_lo_done, j * CH + (NB * CH * layer + k + 1)))
                    up(slot, j + (NB * layer + 1), j * 8 + 4 * (base + 2))
                down(1 - slot, NC * (NB - 1) + Y_MLP[layer], lambda k: uT_hi[:, k, :], lambda k: uT_lo[:, k, :],
                     4 * (base + 2 * NB - 1),
                     lambda k: pe.wait_ge(u_lo_done, CH * (NB - 1) + NB * CH * layer + k + 1),
                     turn_out if layer else None)
            turn_out(NC // 2)


_INS = ["x", "positions", "norm_mix", "norm_mlp", "attn_w_qkv", "attn_w_o", "attn_q_gain", "attn_k_gain",
        "attn_lam_q1", "attn_lam_k1", "attn_lam_q2", "attn_lam_k2", "attn_sub_gain", "pool_w", "pool_scale",
        "mlp_w1", "mlp_w2"]
_ONE_LAYER = {"attn_w_qkv", "attn_w_o", "attn_q_gain", "attn_k_gain", "attn_lam_q1", "attn_lam_k1",
              "attn_lam_q2", "attn_lam_k2", "attn_sub_gain", "pool_w", "pool_scale"}


def kernel(**inputs):
    import concourse.bacc as bacc
    from concourse.bass_utils import run_bass_kernel_spmd

    nc = bacc.Bacc("TRN2", target_bir_lowering=False, num_devices=1, dynamic_dma_scratch_size=1024)
    arrays, args = {}, []
    for name in _INS:
        a = np.ascontiguousarray(inputs[name])
        arrays[f"in_{name}"] = a
        ap = nc.dram_tensor(f"in_{name}", a.shape, mybir.dt.from_np(a.dtype), kind="ExternalInput").ap()
        args.append(ap[0] if name in _ONE_LAYER else ap)
    args.append(nc.dram_tensor("out", (1, S, D), F32, kind="ExternalOutput").ap())
    build_trunk(nc, *args)
    r = run_bass_kernel_spmd(nc, [arrays], core_ids=[0])
    return r.results[0]["out"]
```
